# Optimizing a Trainium2 kernel written in Bass

```python
import jax, jax.numpy as jnp
from jax import lax
import numpy as np
import math

D_MODEL = 1024
BATCH = 1
SEQ = 512
DEPTH = 2

MIX_WIDTH = D_MODEL // 2
RET_HEADS = 4
RET_V_DIM = MIX_WIDTH // RET_HEADS
RET_QK_DIM = RET_V_DIM // 2
RET_CHUNK = 128
SC_WIDTH = MIX_WIDTH
SC_KERNEL = 3
CF_WIDTH = MIX_WIDTH
CF_KERNEL = 31
N_BRANCH = 3
D_FF = int(round(8 * D_MODEL / 3 / 256)) * 256
FFN_KERNEL = 3
ROPE_BASE = 10000.0
EPS = 1e-6

IN_SIZES = [RET_HEADS * RET_QK_DIM, RET_HEADS * RET_QK_DIM, MIX_WIDTH, MIX_WIDTH,
            SC_WIDTH, SC_WIDTH, SC_WIDTH, CF_WIDTH, CF_WIDTH, N_BRANCH * D_MODEL]
IN_WIDTH = sum(IN_SIZES)


def rmsnorm(x, g):
    xf = x.astype(jnp.float32)
    y = xf * lax.rsqrt(jnp.mean(xf * xf, axis=-1, keepdims=True) + EPS)
    return (y * g.astype(jnp.float32)).astype(x.dtype)

def layernorm(x, g, b):
    xf = x.astype(jnp.float32)
    mu = jnp.mean(xf, axis=-1, keepdims=True)
    xc = xf - mu
    y = xc * lax.rsqrt(jnp.mean(xc * xc, axis=-1, keepdims=True) + EPS)
    return (y * g.astype(jnp.float32) + b.astype(jnp.float32)).astype(x.dtype)

def causal_dwconv(x, w, b=None):
    K, C = w.shape
    xp = jnp.pad(x, ((0, 0), (K - 1, 0), (0, 0)))
    y = lax.conv_general_dilated(xp, w.astype(x.dtype)[:, None, :], window_strides=(1,),
                                 padding='VALID', dimension_numbers=('NWC', 'WIO', 'NWC'),
                                 feature_group_count=C)
    if b is not None:
        y = y + b.astype(x.dtype)
    return y

def rotary(x, pos):
    half = x.shape[-1] // 2
    inv = ROPE_BASE ** (-jnp.arange(half, dtype=jnp.float32) / half)
    ang = pos.astype(jnp.float32)[:, None] * inv[None, :]
    cos = jnp.cos(ang)[None, :, None, :]
    sin = jnp.sin(ang)[None, :, None, :]
    x1, x2 = x[..., :half], x[..., half:]
    return jnp.concatenate([x1 * cos - x2 * sin, x2 * cos + x1 * sin], axis=-1)

def retention_chunkwise(q, k, v):
    B, S, H, dk = q.shape
    dv = v.shape[-1]
    C = RET_CHUNK
    N = S // C
    gamma = 1.0 - jnp.exp2(-5.0 - jnp.arange(H, dtype=jnp.float32))
    log_g = jnp.log(gamma)
    i = jnp.arange(C, dtype=jnp.float32)
    diff = i[:, None] - i[None, :]
    decay = jnp.where(diff[None] >= 0,
                      jnp.exp(jnp.maximum(diff, 0.0)[None] * log_g[:, None, None]), 0.0)
    zeta = jnp.exp((C - 1.0 - i)[None, :] * log_g[:, None])
    xi = jnp.exp((i + 1.0)[None, :] * log_g[:, None])
    chunk_decay = jnp.exp(C * log_g)

    def chunks(t):
        return t.reshape(B, N, C, H, t.shape[-1]).transpose(0, 3, 1, 2, 4)

    qc, kc, vc = chunks(q), chunks(k), chunks(v)
    scores = jnp.einsum('bhncd,bhnmd->bhncm', qc, kc) * decay[None, :, None]
    o_inner = jnp.einsum('bhncm,bhnme->bhnce', scores, vc)
    kv = jnp.einsum('bhnmd,bhnme->bhnde', kc * zeta[None, :, None, :, None], vc)

    def step(R, kv_n):
        return chunk_decay[None, :, None, None] * R + kv_n, R

    _, R_prev = lax.scan(step, jnp.zeros((B, H, dk, dv), jnp.float32), jnp.moveaxis(kv, 2, 0))
    R_prev = jnp.moveaxis(R_prev, 0, 2)
    o_cross = jnp.einsum('bhncd,bhnde->bhnce', qc, R_prev) * xi[None, :, None, :, None]
    return (o_inner + o_cross).transpose(0, 2, 3, 1, 4).reshape(B, S, H, dv)

def head_groupnorm(o):
    mu = jnp.mean(o, axis=-1, keepdims=True)
    oc = o - mu
    return oc * lax.rsqrt(jnp.mean(oc * oc, axis=-1, keepdims=True) + EPS)

def first_inputs(seed: int = 0) -> dict:
    key = jax.random.key(seed)
    ks = jax.random.split(key, 20)
    f32 = jnp.float32

    def w(k, shape, fan_in):
        return jax.random.normal(k, shape, f32) * (fan_in ** -0.5)

    def gain(k, shape):
        return 1.0 + 0.02 * jax.random.normal(k, shape, f32)

    def small(k, shape):
        return 0.01 * jax.random.normal(k, shape, f32)

    L = DEPTH
    return {
        "x": jax.random.normal(ks[0], (BATCH, SEQ, D_MODEL), f32),
        "norm_mix_pre": gain(ks[1], (L, D_MODEL)),
        "norm_mix_post": gain(ks[2], (L, D_MODEL)),
        "norm_ffn_pre": gain(ks[3], (L, D_MODEL)),
        "norm_ffn_post": gain(ks[4], (L, D_MODEL)),
        "w_in": w(ks[5], (L, D_MODEL, IN_WIDTH), D_MODEL),
        "w_ret_out": w(ks[6], (L, MIX_WIDTH, D_MODEL), MIX_WIDTH),
        "sc_conv_w": w(ks[7], (L, SC_KERNEL, SC_WIDTH), SC_KERNEL),
        "w_sc_out": w(ks[8], (L, SC_WIDTH, D_MODEL), SC_WIDTH),
        "cf_conv_w": w(ks[9], (L, CF_KERNEL, CF_WIDTH), CF_KERNEL),
        "cf_conv_b": small(ks[10], (L, CF_WIDTH)),
        "cf_ln_g": gain(ks[11], (L, CF_WIDTH)),
        "cf_ln_b": small(ks[12], (L, CF_WIDTH)),
        "w_cf_out": w(ks[13], (L, CF_WIDTH, D_MODEL), CF_WIDTH),
        "w_o": w(ks[14], (L, D_MODEL, D_MODEL), D_MODEL),
        "w_up": w(ks[15], (L, D_MODEL, 2 * D_FF), D_MODEL),
        "ffn_conv_w": w(ks[16], (L, FFN_KERNEL, 2 * D_FF), FFN_KERNEL),
        "w_down": w(ks[17], (L, D_FF, D_MODEL), D_FF),
    }

def first_block(x, norm_mix_pre, norm_mix_post, norm_ffn_pre, norm_ffn_post, w_in, w_ret_out,
              sc_conv_w, w_sc_out, cf_conv_w, cf_conv_b, cf_ln_g, cf_ln_b, w_cf_out, w_o,
              w_up, ffn_conv_w, w_down):
    B, S, D = x.shape
    dt = x.dtype
    pos = jnp.arange(S)
    split_idx = [int(c) for c in np.cumsum(IN_SIZES)[:-1]]
    for l in range(DEPTH):
        h = rmsnorm(x, norm_mix_pre[l])
        proj = h @ w_in[l].astype(dt)
        (q, k, v, g_ret, sc_b, sc_c, sc_x, cf_a, cf_b, gate_logits) = jnp.split(proj, split_idx, axis=-1)

        qh = rotary(q.astype(jnp.float32).reshape(B, S, RET_HEADS, RET_QK_DIM), pos)
        kh = rotary(k.astype(jnp.float32).reshape(B, S, RET_HEADS, RET_QK_DIM), pos) * (RET_QK_DIM ** -0.5)
        vh = v.astype(jnp.float32).reshape(B, S, RET_HEADS, RET_V_DIM)
        o = head_groupnorm(retention_chunkwise(qh, kh, vh)).reshape(B, S, MIX_WIDTH).astype(dt)
        y_ret = (jax.nn.silu(g_ret) * o) @ w_ret_out[l].astype(dt)

        u = causal_dwconv(sc_c * sc_x, sc_conv_w[l])
        y_sc = (sc_b * u) @ w_sc_out[l].astype(dt)

        glu = cf_a * jax.nn.sigmoid(cf_b)
        c = causal_dwconv(glu, cf_conv_w[l], cf_conv_b[l])
        c = jax.nn.silu(layernorm(c, cf_ln_g[l], cf_ln_b[l]))
        y_cf = c @ w_cf_out[l].astype(dt)

        gates = jax.nn.sigmoid(gate_logits).reshape(B, S, N_BRANCH, D)
        merged = gates[:, :, 0] * y_ret + gates[:, :, 1] * y_sc + gates[:, :, 2] * y_cf
        x = x + rmsnorm(merged @ w_o[l].astype(dt), norm_mix_post[l])

        h = rmsnorm(x, norm_ffn_pre[l])
        up = causal_dwconv(h @ w_up[l].astype(dt), ffn_conv_w[l])
        gate, val = jnp.split(up, 2, axis=-1)
        f = (jax.nn.silu(gate) * val) @ w_down[l].astype(dt)
        x = x + rmsnorm(f, norm_ffn_post[l])
    return x


CHUNK = 64

GM_WIDTH = 1024
GM_GROUPS = 4
GM_BLOCK = 128

MLA_HEADS = 8
MLA_NOPE = 128
MLA_ROPE = 64
MLA_VDIM = 128
MLA_QK_DIM = MLA_NOPE + MLA_ROPE
MLA_Q_RANK = 384
MLA_KV_RANK = 256
MLA_WIDTH = MLA_HEADS * MLA_VDIM
ROPE_THETA = 10000.0
Q_BLOCK = 128

LRU_WIDTH = 1280
LRU_BLOCKS = 16
LRU_BW = LRU_WIDTH // LRU_BLOCKS
LRU_C = 8.0
CONV_W = 4

IN_SIZES_2 = (GM_WIDTH, GM_WIDTH, GM_WIDTH, MLA_Q_RANK, MLA_KV_RANK, MLA_ROPE, MLA_WIDTH,
            LRU_WIDTH, LRU_WIDTH, D_MODEL, D_MODEL, D_MODEL)
N_IN = sum(IN_SIZES_2)


def _split_points():
    return [int(s) for s in np.cumsum(IN_SIZES_2)[:-1]]

def rmsnorm_2(x, g):
    xf = x.astype(jnp.float32)
    y = xf * lax.rsqrt(jnp.mean(xf * xf, axis=-1, keepdims=True) + EPS)
    return (y * g.astype(jnp.float32)).astype(x.dtype)

def layernorm_2(x, g, b):
    xf = x.astype(jnp.float32)
    mu = jnp.mean(xf, axis=-1, keepdims=True)
    var = jnp.mean(jnp.square(xf - mu), axis=-1, keepdims=True)
    y = (xf - mu) * lax.rsqrt(var + EPS)
    return (y * g.astype(jnp.float32) + b.astype(jnp.float32)).astype(x.dtype)

def rope(t, cos, sin):
    half = t.shape[-1] // 2
    t1, t2 = t[..., :half], t[..., half:]
    return jnp.concatenate([t1 * cos - t2 * sin, t2 * cos + t1 * sin], axis=-1)

def gmlp_spatial(u, v, ln_g, ln_b, ws, bs):
    B, S, _ = v.shape
    v = layernorm_2(v, ln_g, ln_b)
    vb = v.reshape(B, S // GM_BLOCK, GM_BLOCK, GM_GROUPS, GM_WIDTH // GM_GROUPS)
    idx = jnp.arange(GM_BLOCK)
    mask = (idx[None, :] // CHUNK) <= (idx[:, None] // CHUNK)
    ws_m = jnp.where(mask[None], ws, jnp.zeros_like(ws))
    sv = jnp.einsum('gij,bnjgc->bnigc', ws_m, vb) + bs.T[None, None, :, :, None]
    return u * sv.reshape(B, S, GM_WIDTH)

def mla_attention(c_q, c_kv, k_rope_in, q_norm_g, w_uq, kv_norm_g, w_ukv):
    B, S, _ = c_q.shape
    H = MLA_HEADS
    q = (rmsnorm_2(c_q, q_norm_g) @ w_uq).reshape(B, S, H, MLA_QK_DIM)
    kv = (rmsnorm_2(c_kv, kv_norm_g) @ w_ukv).reshape(B, S, H, MLA_NOPE + MLA_VDIM)
    q_nope, q_rope = q[..., :MLA_NOPE], q[..., MLA_NOPE:]
    k_nope, v = kv[..., :MLA_NOPE], kv[..., MLA_NOPE:]

    pos = jnp.arange(S, dtype=jnp.float32)
    inv_freq = ROPE_THETA ** (-jnp.arange(0, MLA_ROPE, 2, dtype=jnp.float32) / MLA_ROPE)
    ang = pos[:, None] * inv_freq[None, :]
    cos = jnp.cos(ang).astype(q.dtype)
    sin = jnp.sin(ang).astype(q.dtype)
    q_rope = rope(q_rope, cos[None, :, None, :], sin[None, :, None, :])
    k_rope = rope(k_rope_in, cos[None], sin[None])

    q = jnp.concatenate([q_nope, q_rope], axis=-1)
    k = jnp.concatenate([k_nope, jnp.broadcast_to(k_rope[:, :, None, :], (B, S, H, MLA_ROPE))], axis=-1)
    scale = 1.0 / math.sqrt(MLA_QK_DIM)
    nb = S // Q_BLOCK
    qb = q.reshape(B, nb, Q_BLOCK, H, MLA_QK_DIM).transpose(1, 0, 2, 3, 4)
    key_chunk = jnp.arange(S) // CHUNK

    def one_block(args):
        qi, bi = args
        s = jnp.einsum('bqhd,bkhd->bhqk', qi, k).astype(jnp.float32) * scale
        q_chunk = (bi * Q_BLOCK + jnp.arange(Q_BLOCK)) // CHUNK
        mask = key_chunk[None, :] <= q_chunk[:, None]
        s = jnp.where(mask[None, None], s, -1e30)
        p = jax.nn.softmax(s, axis=-1).astype(v.dtype)
        return jnp.einsum('bhqk,bkhd->bqhd', p, v)

    o = lax.map(one_block, (qb, jnp.arange(nb)))
    return o.transpose(1, 0, 2, 3, 4).reshape(B, S, MLA_WIDTH)

def rg_lru(x_c, conv_w, conv_b, w_a, b_a, w_x, b_x, lam):
    B, S, C = x_c.shape
    xc = lax.conv_general_dilated(
        x_c, conv_w[:, None, :].astype(x_c.dtype), window_strides=(1,), padding=[(CONV_W - 1, 0)],
        dimension_numbers=('NWC', 'WIO', 'NWC'), feature_group_count=C) + conv_b
    xb = xc.reshape(B, S, LRU_BLOCKS, LRU_BW)
    r = jax.nn.sigmoid(jnp.einsum('bshi,hij->bshj', xb, w_a).reshape(B, S, C) + b_a)
    i = jax.nn.sigmoid(jnp.einsum('bshi,hij->bshj', xb, w_x).reshape(B, S, C) + b_x)
    rf = r.astype(jnp.float32)
    log_a = -LRU_C * rf * jax.nn.softplus(-lam.astype(jnp.float32))
    a = jnp.exp(log_a)
    mult = jnp.sqrt(jnp.maximum(1.0 - jnp.exp(2.0 * log_a), 0.0))
    bterm = mult * (i.astype(jnp.float32) * xc.astype(jnp.float32))

    def combine(e1, e2):
        a1, b1 = e1
        a2, b2 = e2
        return a1 * a2, a2 * b1 + b2

    _, h = lax.associative_scan(combine, (a, bterm), axis=1)
    return h.astype(x_c.dtype)

def second_inputs(seed: int = 0) -> dict:
    key = jax.random.key(seed)
    ks = iter(jax.random.split(key, 32))
    L, D = DEPTH, D_MODEL

    def nrm(shape, scale):
        return jax.random.normal(next(ks), shape, jnp.float32) * scale

    def gain(shape):
        return 1.0 + nrm(shape, 0.02)

    a_init = jax.random.uniform(next(ks), (L, LRU_WIDTH), jnp.float32, 0.9, 0.999)
    s = a_init ** (1.0 / LRU_C)
    lam = jnp.log(s) - jnp.log1p(-s)

    return {
        "x": nrm((BATCH, SEQ, D), 1.0),
        "pre_norm_g": gain((L, D)),
        "w_in": nrm((L, D, N_IN), D ** -0.5),
        "gm_ln_g": gain((L, GM_WIDTH)),
        "gm_ln_b": nrm((L, GM_WIDTH), 0.02),
        "gm_ws": nrm((L, GM_GROUPS, GM_BLOCK, GM_BLOCK), GM_BLOCK ** -0.5),
        "gm_bs": 1.0 + nrm((L, GM_GROUPS, GM_BLOCK), 0.02),
        "mla_q_norm_g": gain((L, MLA_Q_RANK)),
        "mla_w_uq": nrm((L, MLA_Q_RANK, MLA_HEADS * MLA_QK_DIM), MLA_Q_RANK ** -0.5),
        "mla_kv_norm_g": gain((L, MLA_KV_RANK)),
        "mla_w_ukv": nrm((L, MLA_KV_RANK, MLA_HEADS * (MLA_NOPE + MLA_VDIM)), MLA_KV_RANK ** -0.5),
        "lru_conv_w": nrm((L, CONV_W, LRU_WIDTH), CONV_W ** -0.5),
        "lru_conv_b": nrm((L, LRU_WIDTH), 0.01),
        "lru_w_a": nrm((L, LRU_BLOCKS, LRU_BW, LRU_BW), LRU_BW ** -0.5),
        "lru_b_a": nrm((L, LRU_WIDTH), 0.01),
        "lru_w_x": nrm((L, LRU_BLOCKS, LRU_BW, LRU_BW), LRU_BW ** -0.5),
        "lru_b_x": nrm((L, LRU_WIDTH), 0.01),
        "lru_lambda": lam,
        "w_proj_a": nrm((L, GM_WIDTH, D), GM_WIDTH ** -0.5),
        "w_proj_b": nrm((L, MLA_WIDTH, D), MLA_WIDTH ** -0.5),
        "w_proj_c": nrm((L, LRU_WIDTH, D), LRU_WIDTH ** -0.5),
        "w_out": nrm((L, D, D), D ** -0.5),
        "post_norm_g": gain((L, D)),
    }

def second_block(x, pre_norm_g, w_in, gm_ln_g, gm_ln_b, gm_ws, gm_bs, mla_q_norm_g, mla_w_uq,
              mla_kv_norm_g, mla_w_ukv, lru_conv_w, lru_conv_b, lru_w_a, lru_b_a, lru_w_x,
              lru_b_x, lru_lambda, w_proj_a, w_proj_b, w_proj_c, w_out, post_norm_g):
    cuts = _split_points()
    for l in range(DEPTH):
        h = rmsnorm_2(x, pre_norm_g[l])
        proj = h @ w_in[l]
        (u, v, z_a, c_q, c_kv, k_rope, z_b, x_c, z_c,
         g_a, g_b, g_c) = jnp.split(proj, cuts, axis=-1)

        y_a = gmlp_spatial(u, v, gm_ln_g[l], gm_ln_b[l], gm_ws[l], gm_bs[l]) * jax.nn.silu(z_a)
        y_b = mla_attention(c_q, c_kv, k_rope, mla_q_norm_g[l], mla_w_uq[l],
                            mla_kv_norm_g[l], mla_w_ukv[l]) * jax.nn.silu(z_b)
        y_c = rg_lru(x_c, lru_conv_w[l], lru_conv_b[l], lru_w_a[l], lru_b_a[l],
                     lru_w_x[l], lru_b_x[l], lru_lambda[l]) * jax.nn.silu(z_c)

        merged = (jax.nn.sigmoid(g_a) * (y_a @ w_proj_a[l])
                  + jax.nn.sigmoid(g_b) * (y_b @ w_proj_b[l])
                  + jax.nn.sigmoid(g_c) * (y_c @ w_proj_c[l]))
        x = x + rmsnorm_2(merged @ w_out[l], post_norm_g[l])
    return x


def setup_inputs(seed=0):
    out = dict(first_inputs(seed))
    for name, value in second_inputs(seed + 1).items():
        if name != "x":
            out[name + "_2"] = value
    return out


def reference(
    x, norm_mix_pre, norm_mix_post, norm_ffn_pre, norm_ffn_post, w_in, w_ret_out, sc_conv_w,
    w_sc_out, cf_conv_w, cf_conv_b, cf_ln_g, cf_ln_b, w_cf_out, w_o, w_up, ffn_conv_w, w_down,
    pre_norm_g_2, w_in_2, gm_ln_g_2, gm_ln_b_2, gm_ws_2, gm_bs_2, mla_q_norm_g_2, mla_w_uq_2,
    mla_kv_norm_g_2, mla_w_ukv_2, lru_conv_w_2, lru_conv_b_2, lru_w_a_2, lru_b_a_2, lru_w_x_2,
    lru_b_x_2, lru_lambda_2, w_proj_a_2, w_proj_b_2, w_proj_c_2, w_out_2, post_norm_g_2,
):
    x = first_block(
        x, norm_mix_pre, norm_mix_post, norm_ffn_pre, norm_ffn_post, w_in, w_ret_out, sc_conv_w,
        w_sc_out, cf_conv_w, cf_conv_b, cf_ln_g, cf_ln_b, w_cf_out, w_o, w_up, ffn_conv_w,
        w_down,
    )
    return second_block(
        x, pre_norm_g_2, w_in_2, gm_ln_g_2, gm_ln_b_2, gm_ws_2, gm_bs_2, mla_q_norm_g_2,
        mla_w_uq_2, mla_kv_norm_g_2, mla_w_ukv_2, lru_conv_w_2, lru_conv_b_2, lru_w_a_2,
        lru_b_a_2, lru_w_x_2, lru_b_x_2, lru_lambda_2, w_proj_a_2, w_proj_b_2, w_proj_c_2,
        w_out_2, post_norm_g_2,
    )


_drawn_inputs = setup_inputs


def setup_inputs(seed=0):
    import zlib

    import numpy as np

    out = dict(_drawn_inputs(seed))
    spreads = {}
    factors = {'cf_ln_b': 6.903,
     'pre_norm_g_2': 3.065,
     'gm_ln_g_2': 8.0,
     'gm_ln_b_2': 8.0,
     'gm_bs_2': 7.64,
     'mla_q_norm_g_2': 8.0,
     'mla_kv_norm_g_2': 8.0,
     'lru_conv_b_2': 22.772,
     'lru_b_a_2': 64.0,
     'lru_b_x_2': 64.0,
     'post_norm_g_2': 4.797}
    for name, (base, spread) in spreads.items():
        noise = np.random.default_rng([zlib.crc32(name.encode()), seed]).standard_normal(out[name].shape)
        drawn = base * np.exp(spread * noise) if base else spread * noise
        out[name] = __import__('jax').numpy.asarray(drawn.astype(out[name].dtype))
    for name, factor in factors.items():
        out[name] = (out[name] * factor).astype(out[name].dtype)
    return out
```

```python
from contextlib import ExitStack

import concourse.bass as bass
import numpy as np
from concourse import mybir

F32 = mybir.dt.float32
F32R = mybir.dt.float32r
ALU = mybir.AluOpType
ACT = mybir.ActivationFunctionType
AX_X = mybir.AxisListType.X

P = 128
S = 512
NT = S // P
EPS = 1e-6
MLA_SCALE = (128 + 64) ** -0.5

CH = 1024
D1 = {"q": 0, "k": 256, "v": 512, "g": 1024, "sb": 1536, "sc": 2048, "sx": 2560, "ca": 3072, "cb": 3584,
      "gate": 4096}
D2 = {"u": 0, "v": 1024, "za": 2048, "cq": 3072, "ckv": 3456, "kr": 3712, "zb": 3776, "xc": 4800, "zc": 6080,
      "gate": 7360}


def fm(name, arr, layer, ks, cols, row=0):
    return (name, [(arr, layer, row + k * P, P, cols) for k in ks])


def rng(a, n=P):
    return (a, a + n)


def lru_tiles(j):
    b0, b1 = (j * P) // 80, (j * P + P - 1) // 80
    return list(range((b0 * 80) // P, (b1 * 80 + 79) // P + 1))


def plan():
    out = []
    for l in range(2):
        A = "w_in"

        def one(nm, base, j):
            out.append(fm(f"{nm}{j}", A, l, range(8), rng(base + j * P)))

        for j in range(4):
            one("ca", D1["ca"], j)
            one("cb", D1["cb"], j)
        for j in range(2):
            one("q", D1["q"], j)
            one("k", D1["k"], j)
        for c in range(4):
            out.append((f"v{c}", [(A, l, (2 * c + i) * P, P, rng(D1["v"], 512)) for i in range(2)]))
        for j in range(4):
            one("g", D1["g"], j)
        for j in range(4):
            one("sc", D1["sc"], j)
            one("sx", D1["sx"], j)
            one("sb", D1["sb"], j)
        for b, w in enumerate(("w_ret_out", "w_sc_out", "w_cf_out")):
            for j in range(8):
                one(f"gate{b}_", D1["gate"] + 1024 * b, j)
                if j % 2 == 0:
                    out.append((f"pr{b}_{j}", [(w, l, k * P, P, rng((j + i) * P)) for i in range(2) for k in range(4)]))
        for j in range(8):
            out.append(fm(f"wo{j}", "w_o", l, range(8), rng(j * P)))
        for j in range(22):
            out.append(fm(f"upg{j}", "w_up", l, range(8), rng(j * P)))
            out.append(fm(f"upv{j}", "w_up", l, range(8), rng(2816 + j * P)))
        for j in range(8):
            for p, ks in enumerate((range(0, 8), range(8, 16), range(16, 22))):
                out.append(fm(f"dn{j}_{p}", "w_down", l, ks, rng(j * P)))
    for l in range(2):
        A = "w_in_2"

        def one(nm, base, j):
            out.append(fm(f"{nm}{j}", A, l, range(8), rng(base + j * P)))

        for j in range(3):
            one("cq", D2["cq"], j)
        for j in range(2):
            one("ckv", D2["ckv"], j)
        out.append(("kr", [(A, l, k * P, P, rng(D2["kr"], 64)) for k in range(8) for _ in range(2)]))
        for p in range(2):
            out.append((f"qr{p}", [("mla_w_uq_2", l, k * P, P, rng(h * 192 + 128, 64))
                                   for j in (2 * p, 2 * p + 1) for k in range(3) for h in (2 * j, 2 * j + 1)]))
        for p in range(2):
            out.append((f"vb{p}", [("mla_w_ukv_2", l, k * P, P, rng(h * 256 + 128))
                                   for k in range(2) for h in range(4 * p, 4 * p + 4)]))
        for h in range(8):
            out.append((f"qk{h}", [("mla_w_uq_2", l, k * P, P, rng(h * 192)) for k in range(3)]
                        + [("mla_w_ukv_2", l, k * P, P, rng(h * 256)) for k in range(2)]))
            one("zb", D2["zb"], h)

        def proj(nm, w, nk, b):
            for j in range(8):
                one(f"gate{nm}_", D2["gate"] + 1024 * b, j)
                if nk == 8:
                    out.append(fm(f"pr{nm}_{j}", w, l, range(8), rng(j * P)))
                else:
                    out.append(fm(f"pr{nm}_{j}", w, l, range(5), rng(j * P)))
                    out.append(fm(f"pr{nm}_{j}+", w, l, range(5, 10), rng(j * P)))

        proj("b", "w_proj_b_2", 8, 1)
        for n in range(2):
            for c in range(4):
                out.append((f"va{n}_{c}", [(A, l, (2 * c + i) * P, P, rng(D2["v"] + 512 * n, 512)) for i in range(2)]))
        for j in range(8):
            one("u", D2["u"], j)
            one("za", D2["za"], j)
        proj("a", "w_proj_a_2", 8, 0)
        for h in range(2):
            for j in range(5 * h, 5 * h + 5):
                one("xc", D2["xc"], j)
            for j in range(5 * h, 5 * h + 5):
                out.append((f"lru{j}", [(w, l, i, j, "lru") for w in ("lru_w_a_2", "lru_w_x_2") for i in lru_tiles(j)]))
                one("zc", D2["zc"], j)
        proj("c", "w_proj_c_2", 10, 2)
        for j in range(8):
            out.append(fm(f"wo2_{j}", "w_out_2", l, range(8), rng(j * P)))
    return out


def width(chunk):
    return sum(P if p[4] == "lru" else p[4][1] - p[4][0] for p in chunk[1])


def vec_map(items):
    at, out = 0, {}
    for name, n in items:
        out[name] = at
        at += n
    return out, at


V1, NV1 = vec_map([("pre", 8), ("post", 8), ("fpre", 8), ("fpost", 8), ("scw", 12), ("cfw", 124), ("cfb", 4),
                   ("lng", 4), ("lnb", 4), ("fcw", 132)])
V2, NV2 = vec_map([("pre", 8), ("post", 8), ("qg", 3), ("kvg", 2), ("cw", 40), ("cb", 10), ("ba", 10), ("bx", 10),
                   ("lam", 10)])
NV = max(NV1, NV2)


class Engine:

    def __init__(self, e, sem):
        self.e, self.sem, self.n, self.seen = e, sem, 0, {}

    def _wait(self, waits):
        for w in waits:
            if w is None:
                continue
            if isinstance(w, list):
                self._wait(w)
                continue
            sem, value = w
            if self.seen.get(id(sem), 0) < value:
                self.seen[id(sem)] = value
                self.e.wait_ge(sem, value)

    def quiet(self, fn, *waits):
        self._wait(waits)
        fn(self.e)

    def do(self, fn, *waits):
        self._wait(waits)
        self.n += 1
        fn(self.e).then_inc(self.sem, 1)
        return (self.sem, self.n)

    def dma(self, fn, sem, value, *waits):
        self._wait(waits)
        fn(self.e).then_inc(sem, 16)
        return (sem, value)


class Ring:

    def __init__(self, bufs, *toks):
        self.bufs = list(bufs)
        self.idle = [(i, list(toks)) for i in range(len(self.bufs))]

    def take(self):
        i, w = self.idle.pop(0)
        return i, self.bufs[i], w

    def free(self, i, *toks):
        self.idle.append((i, list(toks)))


def build(nc, x_in, wst, vec, cst, tab, gmb, out):
    chunks = plan()
    ctx = ExitStack()
    with ctx:
        def sb(name, shape, dt):
            return ctx.enter_context(nc.sbuf_tensor(name, shape, dt))

        def sem(name):
            return ctx.enter_context(nc.semaphore(name))

        NB = 69
        NRAW, NSP, LA = 4, 4, 2
        base = (nc.sbuf_base + 31) // 32 * 32
        sb("arena", [P, NB * S + 16], F32)
        X = sb("X", [P, 8 * S], F32)
        raw = sb("raw", [P, NRAW, CH], F32)
        wh = sb("wh", [P, NSP, CH], F32R)
        wl = sb("wl", [P, NSP, CH], F32R)
        vt = sb("vt", [P, 2, NV], F32)
        ct = sb("ct", [P, 3, P], F32)
        sm = sb("sm", [P, 160], F32)
        sm2 = sb("sm2", [P, 2, 20], F32)
        ps = ctx.enter_context(nc.psum_tensor("ps", [P, 8, S], F32))
        ident, ones, perm = ct[:, 0, :], ct[:, 1, :], ct[:, 2, :]

        pe, act, dve, pool = (Engine(e, sem("s_" + n)) for e, n in (
            (nc.tensor, "pe"), (nc.scalar, "act"), (nc.vector, "dve"), (nc.gpsimd, "pool")))
        sp = Engine(nc.sync, None)
        s_raw = [sem(f"s_raw{i}") for i in range(NRAW)]
        n_sem = [0]

        def load(eng, dst, src, *waits):
            n_sem[0] += 1
            return eng.dma(lambda e: e.dma_start(dst, src), sem(f"s_ld{n_sem[0]}"), 16, *waits)

        views = {}

        def view(kind, dt, col, n):
            name = f"{kind}{col}_{n}"
            if name not in views:
                views[name] = nc.alloc_sbuf_tensor_at(name, [P, n], dt, offset=base + 4 * col)[:, :]
            return views[name]

        def F(i, n=1):
            return view("f", F32, i * S, n * S)

        def R(i):
            return view("r", F32R, i * S, S)

        def xt(j):
            return X[:, j * S:(j + 1) * S]

        banks = Ring([ps[:, i, :] for i in range(8)])

        class Weights:
            def __init__(self):
                self.loaded = self.cut = self.opened = 0
                self.split_tok, self.closed = {}, {}

            def load(self):
                c = self.loaded
                self.loaded += 1
                s = c % NRAW
                w = width(chunks[c])
                sp.dma(lambda e: e.dma_start(raw[:, s, 0:w], wst[c, :, 0:w]), s_raw[s], 16 * (c // NRAW + 1),
                       self.split_tok.get(c - NRAW))

            def split(self):
                c = self.cut
                self.cut += 1
                r, s, w = c % NRAW, c % NSP, width(chunks[c])
                assert c < NSP or c - NSP in self.closed, "a split buffer is still in use"
                here = (s_raw[r], 16 * (c // NRAW + 1))
                a = act.do(lambda e: e.copy(wh[:, s, 0:w], raw[:, r, 0:w]), here, self.closed.get(c - NSP))
                b = dve.do(lambda e: e.tensor_tensor(wl[:, s, 0:w], raw[:, r, 0:w], wh[:, s, 0:w].bitcast(F32),
                                                     ALU.subtract), here, a)
                self.split_tok[c] = [a, b]
                if self.loaded < len(chunks):
                    self.load()

            def open(self, name):
                c = self.opened
                assert chunks[c][0] == name, (chunks[c][0], name)
                self.opened += 1
                while self.cut <= min(c + LA, len(chunks) - 1):
                    self.split()
                pump()
                s = c % NSP
                return c, wh[:, s, :], wl[:, s, :], self.split_tok[c]

            def close(self, c, tok):
                self.closed[c] = tok

        later = []

        def pump(n=2):
            for _ in range(min(n, len(later))):
                later.pop(0)()

        def flush():
            while later:
                later.pop(0)()

        W = Weights()

        def mm(o, a, b, start, stop, *waits, sig=False):
            f = lambda e: e.matmul(o, a, b, start=start, stop=stop, skip_group_check=True)
            return pe.do(f, *waits) if sig else pe.quiet(f, *waits)

        def three(o, ah, al, bh, bl, start, stop, *waits, sig=False):
            mm(o, ah, bh, start, False, *waits)
            mm(o, ah, bl, False, False)
            return mm(o, al, bh, False, stop, sig=stop or sig)

        def group(o, ch, cl, cols, xs, waits, start=True, stop=True):
            tok = None
            for i, (c, (xh, xl, xw)) in enumerate(zip(cols, xs)):
                tok = three(o, ch[:, c:c + P], cl[:, c:c + P], xh, xl, start and i == 0,
                            stop and i == len(cols) - 1, waits, xw, sig=i == len(cols) - 1)
            return tok

        def fm_tile(name, xs):
            c, h, l, wt = W.open(name)
            i, o, bw = banks.take()
            t = group(o, h, l, [k * P for k in range(len(xs))], xs, [wt, bw])
            W.close(c, t)
            return i, o, t

        def split_tile(f, h, l, *waits):
            a = act.do(lambda e: e.copy(h, f), *waits)
            b = dve.do(lambda e: e.tensor_tensor(l, f, h.bitcast(F32), ALU.subtract), a, *waits)
            return [a, b]

        def rsqrt_cols(accs, D, wacc):
            i, o, bw = banks.take()
            n = 0
            for a in accs:
                for t in range(NT):
                    tok = mm(o[:, n:n + 1], a[:, t * P:(t + 1) * P], ones[:, 0:1], True, True, bw, wacc, consts, sig=True)
                    n += 1
            j, q, sw = small.take()
            k, r, rw = small.take()
            v = dve.do(lambda e: e.tensor_scalar(q[:, 0:n], o[:, 0:n], 1.0 / D, EPS, ALU.mult, ALU.add), tok, sw)
            banks.free(i, v)
            p = pool.do(lambda e: e.tensor_tensor(r[:, 0:n], q[:, 0:n], half[:, 0:n], ALU.pow), v, rw, consts)
            small.free(j, p)
            return k, r, p

        def spread(r, c0, tok):
            i, o, bw = banks.take()
            for t in range(NT):
                tk = mm(o[:, t * P:(t + 1) * P], r[:, c0 + t:c0 + t + 1].to_broadcast([P, P]), ident, True, True, bw,
                        tok, sig=(t == NT - 1))
            return i, o, tk

        def add_squares(tiles, acc, toks, tmp):
            t = None
            for j, f in enumerate(tiles):
                if j == 0:
                    t = act.do(lambda e, f=f: e.activation(acc, f, ACT.Square), toks[j])
                    continue
                i, q, w = tmp.take()
                a = act.do(lambda e, f=f, q=q: e.activation(q, f, ACT.Square), toks[j], w)
                t = pool.do(lambda e, q=q: e.tensor_tensor(acc, acc, q, ALU.add), a, t)
                tmp.free(i, t)
            return t

        half = sm[:, 144:160]
        small = Ring([sm[:, 16 * i:16 * i + 16] for i in range(8)])
        h0 = dve.do(lambda e: e.memset(half, -0.5))
        c0 = load(sp, ct[:, :, :].rearrange("p a b -> p (a b)"), cst)
        xtok = [load(sp, X[:, 2 * j * S:(2 * j + 2) * S], x_in[:, 2 * j * S:(2 * j + 2) * S]) for j in range(4)]
        xtok = [[xtok[j // 2]] for j in range(8)]
        consts = [h0, c0]
        vtok = [None] * 4
        vtok[0] = load(sp, vt[:, 0, :], vec[0])
        for _ in range(NRAW):
            W.load()
        last_vec = [[], []]

        def norm_into(tiles, toks, gain, hs, ls, tmp, wfree, D, vw):
            ia, acc, aw = tmp.take()
            t = add_squares(tiles, acc, [[toks[j], aw] for j in range(len(tiles))], tmp)
            k, r, p = rsqrt_cols([acc], D, t)
            tmp.free(ia, (pe.sem, pe.n))
            i, o, tk = spread(r, 0, p)
            small.free(k, tk)
            res = []
            for j, f in enumerate(tiles):
                it, q, w = tmp.take()
                a = dve.do(lambda e, f=f, q=q, j=j: e.scalar_tensor_tensor(
                    out=q, in0=f, scalar=gain[:, j:j + 1], in1=o, op0=ALU.mult, op1=ALU.mult), tk, w, toks[j], vw)
                s = split_tile(q, hs[j], ls[j], a, wfree)
                tmp.free(it, *s)
                res.append((hs[j], ls[j], s))
            banks.free(i, a)
            return res

        def residual(names, xs_parts, ybase, gain, tmp, wy, vw):
            ia, acc, aw = tmp.take()
            ytok, t = [], None
            for j in range(8):
                i, o, tk = names(j)
                y = F(ybase + j)
                a = act.do(lambda e, y=y, o=o: e.copy(y, o), tk, wy)
                if j == 0:
                    b = t = act.do(lambda e, o=o: e.activation(acc, o, ACT.Square), tk, aw)
                else:
                    iq, q, w = tmp.take()
                    b = act.do(lambda e, q=q, o=o: e.activation(q, o, ACT.Square), tk, w)
                    t = dve.do(lambda e, q=q: e.tensor_tensor(acc, acc, q, ALU.add), b, t)
                    tmp.free(iq, t)
                banks.free(i, b)
                ytok.append(a)
            k, r, p = rsqrt_cols([acc], 1024, t)
            tmp.free(ia, (pe.sem, pe.n))
            i, o, tk = spread(r, 0, p)
            small.free(k, tk)
            for j in range(8):
                y = F(ybase + j)
                a = dve.do(lambda e, y=y, j=j: e.scalar_tensor_tensor(
                    out=y, in0=y, scalar=gain[:, j:j + 1], in1=o, op0=ALU.mult, op1=ALU.mult), tk, ytok[j], vw)
                xtok[j] = [dve.do(lambda e, y=y, j=j: e.tensor_tensor(xt(j), xt(j), y, ALU.add), a, xtok[j])]
            banks.free(i, a)

        def gate_proj(b, gname, pname, ys, M, tmp, xs, wm, kind):
            pr = None
            for j in range(8):
                ig, og, tg = fm_tile(f"gate{gname}_{j}", xs)
                if kind == "pair":
                    if j % 2 == 0:
                        pr = W.open(f"pr{pname}_{j}")
                    ip, op, bw = banks.take()
                    c, h, l, wt = pr
                    tp = group(op, h, l, [(j % 2 * 4 + k) * P for k in range(4)], ys, [wt, bw])
                    if j % 2:
                        W.close(c, tp)
                else:
                    ip, op, bw = banks.take()
                    n = len(ys) if len(ys) == 8 else 5
                    for k0 in range(0, len(ys), n):
                        c, h, l, wt = W.open(f"pr{pname}_{j}" + ("+" if k0 else ""))
                        tp = group(op, h, l, [k * P for k in range(n)], ys[k0:k0 + n], [wt, bw], k0 == 0,
                                   k0 + n == len(ys))
                        W.close(c, tp)
                it, q, w = tmp.take()
                a = act.do(lambda e, q=q, og=og: e.activation(q, og, ACT.Sigmoid), tg, w)
                banks.free(ig, a)
                if b == 0:
                    m = dve.do(lambda e, q=q, op=op, j=j: e.tensor_tensor(F(M + j), q, op, ALU.mult), a, tp, wm)
                    mtok[j] = [m]
                    banks.free(ip, m)
                    tmp.free(it, m)
                else:
                    m = dve.do(lambda e, q=q, op=op: e.tensor_tensor(q, q, op, ALU.mult), a, tp)
                    banks.free(ip, m)
                    g = pool.do(lambda e, q=q, j=j: e.tensor_tensor(F(M + j), F(M + j), q, ALU.add), m, mtok[j])
                    mtok[j] = [g]
                    tmp.free(it, g)
            return tp

        mtok = [None] * 8

        def rope(i, o, tk, dst, cosF, sinF, tmp, *waits):
            iq, q, w = tmp.take()
            a = act.do(lambda e: e.copy(q, o), tk, w)
            banks.free(i, a)
            ir, r, bw = banks.take()
            tr = mm(r, perm, q, True, True, a, bw, consts, sig=True)
            b = pool.do(lambda e: e.tensor_tensor(dst, q, cosF, ALU.mult), a, *waits)
            c = dve.do(lambda e: e.tensor_tensor(q, r, sinF, ALU.mult), tr, b, *waits)
            banks.free(ir, c)
            d = pool.do(lambda e: e.tensor_tensor(dst, dst, q, ALU.add), c, b)
            tmp.free(iq, d)
            return d

        def mark():
            return [(e.sem, e.n) for e in (pe, act, dve, pool)]

        tri = [0, 512, 896, 1152]

        for l in range(2):
            vi = l % 2
            v = vt[:, vi, :]
            vw = vtok[l]
            temps = Ring([F(i) for i in range(62, 69)])
            start = mark() if l else []


            def vc(name, n=0):
                return v[:, V1[name] + n:]

            H, L = [R(j) for j in range(8)], [R(8 + j) for j in range(8)]
            xs = norm_into([xt(j) for j in range(8)], xtok, vc("pre"), H, L, temps, start, 1024, vw)
            cs = [load(pool, F(52 + i), tab[:, i * S:(i + 1) * S], start) for i in range(2)]
            dec = [load(pool, F(54 + i), tab[:, (2 + i) * S:(3 + i) * S], start) for i in range(4)]
            vtok[l + 1] = load(pool, vt[:, 1 - vi, :], vec[l + 1], start)

            gtok = []
            for j in range(4):
                ia, oa, ta = fm_tile(f"ca{j}", xs)
                ib, ob, tb = fm_tile(f"cb{j}", xs)
                it, q, w = temps.take()
                a = act.do(lambda e: e.activation(q, ob, ACT.Sigmoid), tb, w)
                banks.free(ib, a)
                g = dve.do(lambda e: e.tensor_tensor(F(16 + j), q, oa, ALU.mult), a, ta, start)
                banks.free(ia, g)
                temps.free(it, g)
                gtok.append(g)
            ctok = [None] * 4

            def tap(k, j):
                G, C = F(16 + j), F(20 + j)
                w = vc("cfw", 31 * j + k)
                s = 30 - k
                if s == 0:
                    ctok[j] = act.do(lambda e: e.activation(C, G, ACT.Identity, bias=vc("cfb", j)[:, 0:1],
                                                            scale=w[:, 0:1]), gtok[j], vw, start)
                else:
                    ctok[j] = dve.do(lambda e: e.scalar_tensor_tensor(
                        out=C[:, s:S], in0=G[:, 0:S - s], scalar=w[:, 0:1], in1=C[:, s:S], op0=ALU.mult,
                        op1=ALU.add), ctok[j])

            for k in range(30, -1, -1):
                for j in range(4):
                    later.append(lambda k=k, j=j: tap(k, j))

            QK = []
            for j in range(2):
                for m, nm in enumerate("qk"):
                    i, o, tk = fm_tile(f"{nm}{j}", xs)
                    QK.append(rope(i, o, tk, F(48 + 2 * m + j), F(52), F(53), temps, cs, start))
            vb = [banks.take() for _ in range(NT)]
            for c in range(4):
                n, h, lo, wt = W.open(f"v{c}")
                for t in range(NT):
                    for i in range(2):
                        k = 2 * c + i
                        ts = slice(t * P, (t + 1) * P)
                        tk = three(vb[t][1], H[k][:, ts], L[k][:, ts], h[:, i * S:(i + 1) * S],
                                   lo[:, i * S:(i + 1) * S], k == 0, k == 7, wt, vb[t][2], xs[k][2],
                                   sig=i == 1)
                    if c == 3:
                        a = act.do(lambda e, t=t: e.copy(F(58 + t), vb[t][1]), tk, start)
                        banks.free(vb[t][0], a)
                        if t == 0:
                            V = []
                        V.append(a)
                W.close(n, tk)
            sg = []
            otok, sq = [], []
            Sb = Ring([view("f", F32, 24 * S + 1280 * i, 1280) for i in range(2)], start)
            for h in range(4):
                ig, og, tg = fm_tile(f"g{h}", xs)
                it, q, w = temps.take()
                a = act.do(lambda e: e.activation(q, og, ACT.Sigmoid), tg, w)
                b = dve.do(lambda e: e.tensor_tensor(F(44 + h), q, og, ALU.mult), a, start)
                temps.free(it, b)
                banks.free(ig, b)
                sg.append(b)
                pr = slice(64 * (h % 2), 64 * (h % 2) + 64)
                si, sbuf, sw = Sb.take()
                st = []
                for i in range(NT):
                    ib, o, bw = banks.take()
                    n = S - P * i
                    tk = mm(o[:, 0:n], F(50 + h // 2)[pr, i * P:(i + 1) * P], F(48 + h // 2)[pr, i * P:S], True, True,
                            bw, QK, sig=True)
                    st.append(dve.do(lambda e, o=o, n=n, i=i: e.tensor_tensor(
                        sbuf[:, tri[i]:tri[i] + n], o[:, 0:n], F(54 + h)[:, 0:n], ALU.mult), tk, sw, dec))
                    banks.free(ib, st[-1])
                io, o, bw = banks.take()
                for i in range(NT):
                    tk = mm(o[:, i * P:S], F(58 + i)[:, h * P:(h + 1) * P], sbuf[:, tri[i]:tri[i] + S - P * i], i == 0,
                            i == NT - 1, bw, V, st[i], sig=(i == NT - 1))
                Sb.free(si, tk)
                ot = act.do(lambda e: e.copy(F(40 + h), o), tk, start)
                banks.free(io, ot)
                im, m, bw = banks.take()
                tm = mm(m, ones, F(40 + h), True, True, bw, ot, sig=True)
                oc = dve.do(lambda e: e.scalar_tensor_tensor(out=F(40 + h), in0=m, scalar=-1.0 / P, in1=F(40 + h),
                                                             op0=ALU.mult, op1=ALU.add), tm)
                banks.free(im, oc)
                otok.append(oc)
            ret_done = [(pe.sem, pe.n), (dve.sem, dve.n)]
            sqt = []
            for h in range(4):
                it, q, w = temps.take()
                sqt.append((it, q, act.do(lambda e: e.activation(q, F(40 + h), ACT.Square), otok[h], w)))
            kk, r, p = rsqrt_cols([q for _, q, _ in sqt], P, [t for _, _, t in sqt])
            for it, _, _ in sqt:
                temps.free(it, (pe.sem, pe.n))
            Y = []
            for h in range(4):
                i, o, tk = spread(r, 4 * h, p)
                it, q, w = temps.take()
                a = pool.do(lambda e: e.tensor_tensor(q, F(40 + h), F(44 + h), ALU.mult), w, otok[h], sg[h])
                b = dve.do(lambda e: e.tensor_tensor(q, q, o, ALU.mult), a, tk)
                banks.free(i, b)
                s = split_tile(q, R(40 + h), R(44 + h), b)
                temps.free(it, *s)
                Y.append((R(40 + h), R(44 + h), s))
            small.free(kk, tk)
            Yret = Y

            Ysc = []
            for j in range(4):
                ic, oc, tc = fm_tile(f"sc{j}", xs)
                it, q, w = temps.take()
                a = act.do(lambda e: e.copy(q, oc), tc, w)
                banks.free(ic, a)
                ix, ox, tx = fm_tile(f"sx{j}", xs)
                b = dve.do(lambda e: e.tensor_tensor(q, q, ox, ALU.mult), a, tx)
                banks.free(ix, b)
                iu, u, w = temps.take()
                cw = vc("scw", 3 * j)
                t = act.do(lambda e: e.activation(u, q, ACT.Copy, scale=cw[:, 2:3]), b, w, vw)
                for s in (1, 2):
                    t = dve.do(lambda e, s=s: e.scalar_tensor_tensor(
                        out=u[:, s:S], in0=q[:, 0:S - s], scalar=cw[:, 2 - s:3 - s], in1=u[:, s:S], op0=ALU.mult,
                        op1=ALU.add), t)
                temps.free(it, t)
                ib, ob, tb = fm_tile(f"sb{j}", xs)
                t = dve.do(lambda e: e.tensor_tensor(u, u, ob, ALU.mult), t, tb)
                banks.free(ib, t)
                s = split_tile(u, R(32 + j), R(36 + j), t, start)
                temps.free(iu, *s)
                Ysc.append((R(32 + j), R(36 + j), s))

            M = 48
            tp = gate_proj(0, "0", "0", Yret, M, temps, xs, ret_done, "pair")

            flush()
            ia, acc, aw = temps.take()
            t = pool.do(lambda e: e.tensor_tensor(acc, F(20), F(21), ALU.add), ctok, aw)
            for j in (2, 3):
                t = pool.do(lambda e, j=j: e.tensor_tensor(acc, acc, F(20 + j), ALU.add), t)
            im, m, bw = banks.take()
            tm = mm(m, ones, acc, True, True, bw, t, sig=True)
            xcs = []
            for j in range(4):
                xcs.append(dve.do(lambda e, j=j: e.scalar_tensor_tensor(
                    out=F(20 + j), in0=m, scalar=-1.0 / 512, in1=F(20 + j), op0=ALU.mult, op1=ALU.add), tm))
            banks.free(im, xcs[-1])
            t = add_squares([F(20 + j) for j in range(4)], acc, [[q, tm] for q in xcs], temps)
            kk, r, p = rsqrt_cols([acc], 512, t)
            temps.free(ia, (pe.sem, pe.n))
            i, o, tk = spread(r, 0, p)
            small.free(kk, tk)
            Ycf = []
            for j in range(4):
                C = F(20 + j)
                a = dve.do(lambda e: e.scalar_tensor_tensor(out=C, in0=C, scalar=vc("lng", j)[:, 0:1], in1=o,
                                                            op0=ALU.mult, op1=ALU.mult), tk)
                it, q, w = temps.take()
                b = act.do(lambda e: e.activation(q, C, ACT.Sigmoid, bias=vc("lnb", j)[:, 0:1]), a, w)
                c = dve.do(lambda e: e.scalar_tensor_tensor(out=q, in0=C, scalar=vc("lnb", j)[:, 0:1], in1=q,
                                                            op0=ALU.add, op1=ALU.mult), b)
                s = split_tile(q, R(24 + j), R(28 + j), c, ret_done)
                temps.free(it, *s)
                Ycf.append((R(24 + j), R(28 + j), s))
            banks.free(i, a)
            tp1 = gate_proj(1, "1", "1", Ysc, M, temps, xs, None, "pair")
            tp2 = gate_proj(2, "2", "2", Ycf, M, temps, xs, None, "pair")
            ms = []
            for j in range(8):
                s = split_tile(F(M + j), R(32 + j), R(40 + j), mtok[j], tp1)
                ms.append((R(32 + j), R(40 + j), s))
            residual(lambda j: fm_tile(f"wo{j}", ms), None, 24, vc("post"), temps, tp2, vw)

            xs = norm_into([xt(j) for j in range(8)], xtok, vc("fpre"), H, L, temps, None, 1024, vw)
            ff = mark()
            temps = Ring([F(i) for i in range(60, 69)], ff)
            Fs = []
            for j in range(22):
                gv = []
                for m, nm in enumerate(("upg", "upv")):
                    i, o, tk = fm_tile(f"{nm}{j}", xs)
                    it, q, w = temps.take()
                    cw = vc("fcw", 3 * (22 * m + j))
                    t = act.do(lambda e: e.activation(q, o, ACT.Copy, scale=cw[:, 2:3]), tk, w)
                    for s in (1, 2):
                        t = dve.do(lambda e, s=s: e.scalar_tensor_tensor(
                            out=q[:, s:S], in0=o[:, 0:S - s], scalar=cw[:, 2 - s:3 - s], in1=q[:, s:S], op0=ALU.mult,
                            op1=ALU.add), t)
                    banks.free(i, t)
                    gv.append((it, q, t))
                (ig, g, tg), (iv, u, tu) = gv
                it, q, w = temps.take()
                a = act.do(lambda e: e.activation(q, g, ACT.Sigmoid), tg, w)
                b = pool.do(lambda e: e.tensor_tensor(u, g, u, ALU.mult), tg, tu)
                c = dve.do(lambda e: e.tensor_tensor(q, q, u, ALU.mult), a, b)
                temps.free(ig, a, b)
                temps.free(iv, c)
                s = split_tile(q, R(16 + j), R(38 + j), c, ff)
                temps.free(it, *s)
                Fs.append((R(16 + j), R(38 + j), s))

            def down(j):
                i, o, bw = banks.take()
                for p, ks in enumerate((range(0, 8), range(8, 16), range(16, 22))):
                    c, h, lo, wt = W.open(f"dn{j}_{p}")
                    tk = group(o, h, lo, [k * P for k in range(len(ks))], [Fs[k] for k in ks], [wt, bw], p == 0, p == 2)
                    W.close(c, tk)
                return i, o, tk

            residual(down, None, 0, vc("fpost"), temps, (pe.sem, pe.n), vw)

        for l in range(2):
            vi = l % 2
            v = vt[:, vi, :]
            vw = vtok[2 + l]
            start = mark()
            temps = Ring([F(i) for i in list(range(61, 69)) + [46, 52, 53, 54, 55, 56, 57, 58]], start)

            def vc(name, n=0):
                return v[:, V2[name] + n:]

            H, L = [R(j) for j in range(8)], [R(8 + j) for j in range(8)]
            xs = norm_into([xt(j) for j in range(8)], xtok, vc("pre"), H, L, temps, start, 1024, vw)
            cs = [load(pool, F(59 + i), tab[:, i * S:(i + 1) * S], start) for i in range(2)]
            if l == 0:
                vtok[3] = load(pool, vt[:, 1, :], vec[3], start)

            lam = vc("lam")[:, 0:10]
            q = [small.take() for _ in range(5)]
            u, d, z, z2, pp = (a[1][:, 0:10] for a in q)
            cc = sm2[:, vi, :]
            w5 = [a[2] for a in q]
            t = act.do(lambda e: e.activation(u, lam, ACT.Abs), vw, w5)
            t = act.do(lambda e: e.activation(u, u, ACT.Exp, scale=-1.0), t)
            t = dve.do(lambda e: e.tensor_scalar(d, u, 2.0, None, ALU.add), t, w5)
            t = dve.do(lambda e: e.reciprocal(d, d), t)
            t = dve.do(lambda e: e.tensor_tensor(z, u, d, ALU.mult), t)
            t = dve.do(lambda e: e.tensor_tensor(z2, z, z, ALU.mult), t)
            t = dve.do(lambda e: e.tensor_scalar(pp, z2, 1.0 / 17, None, ALU.mult), t)
            for n in (15, 13, 11, 9, 7, 5, 3):
                t = dve.do(lambda e, n=n: e.scalar_tensor_tensor(out=pp, in0=pp, scalar=1.0 / n, in1=z2, op0=ALU.add,
                                                                 op1=ALU.mult), t)
            t = dve.do(lambda e: e.scalar_tensor_tensor(out=pp, in0=pp, scalar=1.0, in1=z, op0=ALU.add, op1=ALU.mult), t)
            t = dve.do(lambda e: e.tensor_scalar(d, lam, -1.0, 0.0, ALU.mult, ALU.max), t)
            t = dve.do(lambda e: e.scalar_tensor_tensor(out=d, in0=pp, scalar=2.0, in1=d, op0=ALU.mult, op1=ALU.add), t)
            t = dve.do(lambda e: e.tensor_scalar(cc[:, 0:10], d, -8.0, None, ALU.mult), t, start)
            t = dve.do(lambda e: e.tensor_scalar(cc[:, 10:20], d, -16.0, None, ALU.mult), t)
            cctok = t
            for a in q:
                small.free(a[0], t)

            cqt, kvt = [], []
            for j in range(3):
                i, o, tk = fm_tile(f"cq{j}", xs)
                cqt.append(act.do(lambda e: e.copy(F(47 + j), o), tk, start))
                banks.free(i, cqt[-1])
            for j in range(2):
                i, o, tk = fm_tile(f"ckv{j}", xs)
                kvt.append(act.do(lambda e: e.copy(F(50 + j), o), tk, start))
                banks.free(i, kvt[-1])
            i, o, tk = fm_tile("kr", xs)
            krt = rope(i, o, tk, F(42), F(59), F(60), temps, cs, start)
            qs = norm_into([F(47 + j) for j in range(3)], cqt, vc("qg"), [R(32 + j) for j in range(3)],
                           [R(35 + j) for j in range(3)], temps, start, 384, vw)
            kvs = norm_into([F(50 + j) for j in range(2)], kvt, vc("kvg"), [R(38 + j) for j in range(2)],
                            [R(40 + j) for j in range(2)], temps, start, 256, vw)
            raw_free = mark()
            qrt = []
            for p in range(2):
                c, h, lo, wt = W.open(f"qr{p}")
                for j in range(2):
                    i, o, bw = banks.take()
                    tk = group(o, h, lo, [(3 * j + k) * P for k in range(3)], qs, [wt, bw])
                    qrt.append(rope(i, o, tk, F(43 + 2 * p + j), F(59), F(60), temps, cs, start, raw_free if 2 * p + j == 3 else None))
                W.close(c, tk)
            V = []
            for n in range(2):
                c, h, lo, wt = W.open(f"vb{n}")
                for t in range(NT):
                    ib, o, bw = banks.take()
                    ts = slice(t * P, (t + 1) * P)
                    for k in range(2):
                        tk = three(o, kvs[k][0][:, ts], kvs[k][1][:, ts], h[:, k * S:(k + 1) * S],
                                   lo[:, k * S:(k + 1) * S], k == 0, k == 1, wt, bw, kvs[k][2])
                    a = act.do(lambda e: e.copy(F(47 + 4 * n + t), o), tk, raw_free, mark())
                    banks.free(ib, a)
                    V.append(a)
                W.close(c, tk)
            head0 = mark()
            qkr = Ring([(F(55), F(56)), (F(57), F(58))], head0)
            PT = Ring([view("f", F32, 59 * S + 1280 * i, 1280) for i in range(2)], head0)
            Pb = Ring([view("f", F32, 64 * S, 1280)], head0)
            temps = Ring([F(67), F(68)], head0)

            def pre(h):
                c, wh_, wl_, wt = W.open(f"qk{h}")
                b, (qn, kn), w = qkr.take()
                i, o, bw = banks.take()
                tq = group(o, wh_, wl_, [k * P for k in range(3)], qs, [wt, bw])
                a = act.do(lambda e: e.copy(qn, o), tq, w)
                banks.free(i, a)
                i2, o2, bw = banks.take()
                tk = group(o2, wh_, wl_, [(3 + k) * P for k in range(2)], kvs, [wt, bw])
                W.close(c, tk)
                d = dve.do(lambda e: e.tensor_copy(kn, o2), tk, w)
                banks.free(i2, d)
                iz, oz, tz = fm_tile(f"zb{h}", xs)
                it, z, w = temps.take()
                s = act.do(lambda e: e.activation(z, oz, ACT.Sigmoid), tz, w)
                s2 = dve.do(lambda e: e.tensor_tensor(z, z, oz, ALU.mult), s)
                banks.free(iz, s2)
                return b, qn, kn, [a, d], it, z, s2

            def scores(h, pr):
                b, qn, kn, tk0, _, _, _ = pr
                rows = slice(64 * (h % 2), 64 * (h % 2) + 64)
                ip, pb, pw = Pb.take()
                im, mx, mw = small.take()
                ir, rs, rw = small.take()
                bk, mt = [], []
                for i in range(NT):
                    n = (i + 1) * P
                    ib, o, bw = banks.take()
                    mm(o[:, 0:n], qn[:, i * P:n], kn[:, 0:n], True, False, bw, tk0)
                    tk = mm(o[:, 0:n], F(43 + h // 2)[rows, i * P:n], F(42)[rows, 0:n], False, True, qrt, krt, sig=True)
                    t = dve.do(lambda e, o=o, i=i: e.memset(o[0:64, i * P + 64:(i + 1) * P], -1e30), tk)
                    t = dve.do(lambda e, o=o, i=i, n=n: e.tensor_reduce(mx[:, i:i + 1], o[:, 0:n], AX_X, ALU.max), t, mw)
                    bk.append((ib, o, n))
                    mt.append(t)
                qkr.free(b, tk)
                nb = dve.do(lambda e: e.tensor_scalar(mx[:, 4:8], mx[:, 0:4], -MLA_SCALE, None, ALU.mult), mt)
                ex = []
                offs = [0, 128, 384, 768]
                for i, (ib, o, n) in enumerate(bk):
                    a = act.do(lambda e, o=o, i=i, n=n: e.activation(
                        pb[:, offs[i]:offs[i] + n], o[:, 0:n], ACT.Exp, bias=mx[:, 4 + i:5 + i], scale=MLA_SCALE,
                        accum_out=rs[:, i:i + 1]), nb, pw, rw)
                    banks.free(ib, a)
                    ex.append(a)
                small.free(im, a)
                t = dve.do(lambda e: e.reciprocal(rs[:, 4:8], rs[:, 0:4]), ex)
                nt = []
                for i in range(NT):
                    n = (i + 1) * P
                    nt.append(dve.do(lambda e, i=i, n=n: e.tensor_scalar(
                        pb[:, offs[i]:offs[i] + n], pb[:, offs[i]:offs[i] + n], rs[:, 4 + i:5 + i], None, ALU.mult), t))
                small.free(ir, nt[-1])
                return ip, pb, offs, nt

            def turn(h, pr):
                ip, pb, offs, nt = pr
                it, pt, tw = PT.take()
                ev = []
                for a, ms_ in enumerate(((0,), (1,), (2, 3))):
                    ib, o, bw = banks.take()
                    c = 0
                    for m in ms_:
                        for i in range(m, NT):
                            dst = o[:, c:c + P]
                            src = pb[:, offs[i] + m * P:offs[i] + (m + 1) * P]
                            tk = pe.do(lambda e, dst=dst, src=src: e.transpose(dst, src, ident), bw, nt[i], consts)
                            c += P
                    f = (lambda e, o=o, c=c, a=a: e.tensor_copy(pt[:, tri[a]:tri[a] + c], o[:, 0:c]))
                    g = (lambda e, o=o, c=c, a=a: e.copy(pt[:, tri[a]:tri[a] + c], o[:, 0:c]))
                    ev.append(dve.do(f, tk, tw) if a == 0 else act.do(g, tk, tw))
                    banks.free(ib, ev[-1])
                Pb.free(ip, tk)
                return it, pt, ev

            Yb = []

            def values(h, tr, pr):
                it, pt, ev = tr
                io, o, bw = banks.take()
                for i in range(NT):
                    tk = mm(o[:, i * P:S], F(47 + 4 * (h // 4) + i)[:, (h % 4) * P:(h % 4 + 1) * P],
                            pt[:, tri[i]:tri[i] + S - i * P], i == 0, i == NT - 1, bw, V, ev, sig=(i == NT - 1))
                PT.free(it, tk)
                izt, z, zt = pr[4:]
                t = dve.do(lambda e: e.tensor_tensor(z, z, o, ALU.mult), tk, zt)
                banks.free(io, t)
                s = split_tile(z, R(16 + h), R(24 + h), t, start)
                temps.free(izt, *s)
                Yb.append((R(16 + h), R(24 + h), s))

            cur = pre(0)
            sc = scores(0, cur)
            for h in range(8):
                nxt = pre(h + 1) if h < 7 else None
                tr = turn(h, sc)
                sc = scores(h + 1, nxt) if h < 7 else None
                values(h, tr, cur)
                cur = nxt

            M = 56
            att = mark()
            temps = Ring([F(i) for i in [64, 65, 66, 67, 68] + list(range(46, 56))], att)
            gb = [load(pool, F(40 + 2 * i, 2), gmb[l, :, 2 * i * S:(2 * i + 2) * S], att) for i in range(2)]
            ws = [load(pool, F(44 + i), gmb[l, :, (4 + i) * S:(5 + i) * S], att) for i in range(2)]
            zm = dve.do(lambda e: e.memset(F(44)[64:128, :].rearrange("p (g i) -> p g i", g=4)[:, :, 0:64], 0.0), ws)
            tpb = gate_proj(0, "b", "b", Yb, M, temps, xs, att, "one")

            lnt = []
            for n in range(2):
                vb = [banks.take() for _ in range(NT)]
                for c in range(4):
                    m, h, lo, wt = W.open(f"va{n}_{c}")
                    for t in range(NT):
                        for i in range(2):
                            k = 2 * c + i
                            ts = slice(t * P, (t + 1) * P)
                            tk = three(vb[t][1], H[k][:, ts], L[k][:, ts], h[:, i * S:(i + 1) * S],
                                       lo[:, i * S:(i + 1) * S], k == 0, k == 7, wt, vb[t][2], xs[k][2],
                                   sig=i == 1)
                        if c == 3:
                            a = act.do(lambda e, t=t, n=n: e.copy(F(32 + 2 * t, 2)[:, n * S:(n + 1) * S], vb[t][1]), tk, att)
                            banks.free(vb[t][0], a)
                            lnt.append(a)
                    W.close(m, tk)
            Va = []
            for t in range(NT):
                ist, st, sw = small.take()
                imv, mv, mw = small.take()
                vv = F(32 + 2 * t, 2)
                a = dve.do(lambda e: e.bn_stats(st[:, 0:6], vv[:, 0:S]), lnt[t], lnt[4 + t], sw)
                b = dve.do(lambda e: e.bn_stats(st[:, 6:12], vv[:, S:2 * S]), a)
                b = dve.do(lambda e: e.bn_aggr(mv[:, 0:2], st[:, 0:12]), a, b, mw)
                small.free(ist, b)
                b = dve.do(lambda e: e.tensor_scalar(mv[:, 2:3], mv[:, 1:2], EPS, None, ALU.add), b)
                r = pool.do(lambda e: e.tensor_tensor(mv[:, 3:4], mv[:, 2:3], half[:, 0:1], ALU.pow), b)
                c = dve.do(lambda e: e.scalar_tensor_tensor(out=vv, in0=vv, scalar=mv[:, 0:1], in1=F(40, 2),
                                                            op0=ALU.subtract, op1=ALU.mult), b, gb)
                c = dve.do(lambda e: e.scalar_tensor_tensor(out=vv, in0=vv, scalar=mv[:, 3:4], in1=F(42, 2),
                                                            op0=ALU.mult, op1=ALU.add), c, r)
                small.free(imv, c)
                Va.append(c)
            Ya = []
            for j in range(8):
                iu, ou, tu = fm_tile(f"u{j}", xs)
                iz, oz, tz = fm_tile(f"za{j}", xs)
                io, o, bw = banks.take()
                g = j // 2
                for b in range(NT):
                    tk = mm(o[:, b * P:(b + 1) * P], F(32 + 2 * b, 2)[:, j * P:(j + 1) * P],
                            F(44)[:, g * P:(g + 1) * P], True, True, bw, Va, ws, zm, sig=(b == NT - 1))
                it, q, w = temps.take()
                i2, q2, w2 = temps.take()
                bs = F(45)[:, g * P:(g + 1) * P].unsqueeze(1).to_broadcast([P, NT, P])
                a = dve.do(lambda e: e.tensor_tensor(q[:, :].rearrange("p (b i) -> p b i", b=NT),
                                                     o[:, :].rearrange("p (b i) -> p b i", b=NT), bs, ALU.add),
                           tk, w, ws)
                banks.free(io, a)
                a = dve.do(lambda e: e.tensor_tensor(q, q, ou, ALU.mult), a, tu)
                banks.free(iu, a)
                s = act.do(lambda e: e.activation(q2, oz, ACT.Sigmoid), tz, w2)
                s = dve.do(lambda e: e.tensor_tensor(q2, q2, oz, ALU.mult), s)
                banks.free(iz, s)
                a = pool.do(lambda e: e.tensor_tensor(q, q, q2, ALU.mult), a, s)
                temps.free(i2, a)
                s = split_tile(q, R(16 + j), R(24 + j), a, tpb)
                temps.free(it, *s)
                Ya.append((R(16 + j), R(24 + j), s))
            gate_proj(1, "a", "a", Ya, M, temps, xs, None, "one")

            lru = mark()
            temps = Ring([F(i) for i in [31, 52, 53, 54, 55, 64, 65, 66, 67, 68]], lru)
            Yc = []
            half_done = lru
            for hf in range(2):
                xcs = {}
                for t in range(5):
                    j = 5 * hf + t
                    i, o, tk = fm_tile(f"xc{j}", xs)
                    x_ = F(16 + t)
                    cw = vc("cw", 4 * j)
                    a = act.do(lambda e: e.activation(x_, o, ACT.Identity, bias=vc("cb", j)[:, 0:1],
                                                      scale=cw[:, 3:4]), tk, half_done, vw)
                    for s in (1, 2, 3):
                        a = dve.do(lambda e, s=s: e.scalar_tensor_tensor(
                            out=x_[:, s:S], in0=o[:, 0:S - s], scalar=cw[:, 3 - s:4 - s], in1=x_[:, s:S],
                            op0=ALU.mult, op1=ALU.add), a)
                    banks.free(i, a)
                    s = split_tile(x_, R(21 + t), R(26 + t), a, half_done)
                    xcs[j] = (R(21 + t), R(26 + t), s)
                for t in range(5):
                    j = 5 * hf + t
                    ks = lru_tiles(j)
                    c, h, lo, wt = W.open(f"lru{j}")
                    ia, oa, bw = banks.take()
                    ta = group(oa, h, lo, [k * P for k in range(len(ks))], [xcs[k] for k in ks], [wt, bw])
                    ii, oi, bw = banks.take()
                    ti = group(oi, h, lo, [(len(ks) + k) * P for k in range(len(ks))], [xcs[k] for k in ks], [wt, bw])
                    W.close(c, ti)
                    iz, oz, tz = fm_tile(f"zc{j}", xs)
                    n1, r, w1 = temps.take()
                    n2, q, w2 = temps.take()
                    n3, a_, w3 = temps.take()
                    n4, z, w4 = temps.take()
                    a = act.do(lambda e: e.activation(r, oa, ACT.Sigmoid, bias=vc("ba", j)[:, 0:1]), ta, w1, vw)
                    banks.free(ia, a)
                    b = act.do(lambda e: e.activation(q, oi, ACT.Sigmoid, bias=vc("bx", j)[:, 0:1]), ti, w2)
                    banks.free(ii, b)
                    sz = act.do(lambda e: e.activation(z, oz, ACT.Sigmoid), tz, w4)
                    ea = act.do(lambda e: e.activation(a_, r, ACT.Exp, scale=cc[:, j:j + 1]), a, w3, cctok)
                    e2 = act.do(lambda e: e.activation(r, r, ACT.Exp, scale=cc[:, 10 + j:11 + j]), ea)
                    d = dve.do(lambda e: e.tensor_scalar(r, r, 1.0, None, ALU.min), e2)
                    d = act.do(lambda e: e.activation(r, r, ACT.Sqrt, scale=-1.0, bias=1.0), d)
                    b = pool.do(lambda e: e.tensor_tensor(q, q, F(16 + t), ALU.mult), b)
                    sz = dve.do(lambda e: e.tensor_tensor(z, z, oz, ALU.mult), sz)
                    banks.free(iz, sz)
                    d = dve.do(lambda e: e.tensor_tensor(r, r, q, ALU.mult), d, b)
                    d = dve.do(lambda e: e.tensor_tensor_scan(q, a_, r, 0.0, ALU.mult, ALU.add), d, ea)
                    temps.free(n1, d)
                    temps.free(n3, d)
                    d = dve.do(lambda e: e.tensor_tensor(q, q, z, ALU.mult), d, sz)
                    temps.free(n4, d)
                    s = split_tile(q, R(32 + j), R(42 + j), d, lru)
                    temps.free(n2, *s)
                    Yc.append((R(32 + j), R(42 + j), s))
                half_done = mark()
            tpc = gate_proj(2, "c", "c", Yc, M, temps, xs, None, "one")
            ms = []
            for j in range(8):
                s = split_tile(F(M + j), R(16 + j), R(24 + j), mtok[j], half_done)
                ms.append((R(16 + j), R(24 + j), s))
            residual(lambda j: fm_tile(f"wo2_{j}", ms), None, 32, vc("post"), temps, tpc, vw)

        s_out = sem("s_out")
        for j in range(8):
            sp.dma(lambda e, j=j: e.dma_start(out[:, j * S:(j + 1) * S], xt(j)), s_out, 16 * (j + 1), xtok[j])
        nc.sync.wait_ge(s_out, 16 * 8)


def pack_weights(a):
    chunks = plan()
    out = np.zeros((len(chunks), P, CH), np.float32)
    dense = {}
    for w in ("lru_w_a_2", "lru_w_x_2"):
        d = np.zeros((2, 1280, 1280), np.float32)
        for b in range(16):
            d[:, 80 * b:80 * b + 80, 80 * b:80 * b + 80] = a[w][:, b]
        dense[w] = d
    for n, (_, pieces) in enumerate(chunks):
        c = 0
        for p in pieces:
            if p[4] == "lru":
                w, l, i, j, _ = p
                out[n, :, c:c + P] = dense[w][l, i * P:(i + 1) * P, j * P:(j + 1) * P]
                c += P
            else:
                w, l, r, nr, (c0, c1) = p
                out[n, 0:nr, c:c + c1 - c0] = a[w][l, r:r + nr, c0:c1]
                c += c1 - c0
    return out


def cols(x):
    return x.reshape(-1, P).T


def taps(w):
    k = w.shape[0]
    return w.reshape(k, -1, P).transpose(2, 1, 0).reshape(P, -1)


def pack_vectors(a):
    out = np.zeros((4, P, NV), np.float32)
    for l in range(2):
        for m, parts in ((V1, {"pre": cols(a["norm_mix_pre"][l]), "post": cols(a["norm_mix_post"][l]),
                               "fpre": cols(a["norm_ffn_pre"][l]), "fpost": cols(a["norm_ffn_post"][l]),
                               "scw": taps(a["sc_conv_w"][l]), "cfw": taps(a["cf_conv_w"][l]),
                               "cfb": cols(a["cf_conv_b"][l]), "lng": cols(a["cf_ln_g"][l]),
                               "lnb": cols(a["cf_ln_b"][l]), "fcw": taps(a["ffn_conv_w"][l])}),
                         (V2, {"pre": cols(a["pre_norm_g_2"][l]), "post": cols(a["post_norm_g_2"][l]),
                               "qg": cols(a["mla_q_norm_g_2"][l]), "kvg": cols(a["mla_kv_norm_g_2"][l]),
                               "cw": taps(a["lru_conv_w_2"][l]), "cb": cols(a["lru_conv_b_2"][l]),
                               "ba": cols(a["lru_b_a_2"][l]), "bx": cols(a["lru_b_x_2"][l]),
                               "lam": cols(a["lru_lambda_2"][l])})):
            for name, v in parts.items():
                out[l + (2 if m is V2 else 0), :, m[name]:m[name] + v.shape[1]] = v
    return out


def pack_spatial(a):
    out = np.zeros((2, P, 6 * S), np.float32)
    for l in range(2):
        out[l, :, 0:1024] = np.broadcast_to(a["gm_ln_g_2"][l], (P, 1024))
        out[l, :, 1024:2048] = np.broadcast_to(a["gm_ln_b_2"][l], (P, 1024))
        out[l, :, 2048:2560] = a["gm_ws_2"][l].transpose(2, 0, 1).reshape(P, 512)
        out[l, :, 2560:3072] = np.broadcast_to(a["gm_bs_2"][l].reshape(-1), (P, 512))
    return out


def constants():
    c = np.zeros((P, 3, P), np.float32)
    c[:, 0] = np.eye(P)
    c[:, 1] = 1.0
    for m in range(P):
        if m % 64 < 32:
            c[m + 32, 2, m] = -1.0
        else:
            c[m - 32, 2, m] = 1.0
    t = np.zeros((P, 6, S), np.float32)
    inv = (np.float32(10000.0) ** (-np.arange(32, dtype=np.float32) / np.float32(32))).astype(np.float32)
    ang = np.arange(S, dtype=np.float32)[None, :] * inv[np.arange(P) % 32][:, None]
    t[:, 0] = np.cos(ang)
    t[:, 1] = np.sin(ang)
    diff = np.arange(S)[None, :] - np.arange(P)[:, None]
    for h in range(4):
        lg = np.log(1.0 - 2.0 ** (-5.0 - h))
        t[:, 2 + h] = np.where(diff >= 0, np.exp(np.maximum(diff, 0) * lg), 0.0) * 64 ** -0.5
    return c.reshape(P, 3 * P), t.reshape(P, 6 * S)


def kernel(**inputs):
    import concourse.bacc as _bacc
    from concourse.bass_utils import run_bass_kernel_spmd as _run

    a = {k: np.asarray(v) for k, v in inputs.items()}
    cst, tab = constants()
    arrays = {
        "x_in": np.ascontiguousarray(a["x"][0].T.reshape(8, P, S).transpose(1, 0, 2).reshape(P, 8 * S)),
        "wst": pack_weights(a),
        "vec": pack_vectors(a),
        "cst": cst,
        "tab": tab,
        "gmb": pack_spatial(a),
    }
    nc = _bacc.Bacc("TRN2", target_bir_lowering=False, num_devices=1)
    args = [nc.dram_tensor(n, v.shape, F32, kind="ExternalInput").ap() for n, v in arrays.items()]
    o = nc.dram_tensor("out", (P, 8 * S), F32, kind="ExternalOutput").ap()
    build(nc, *args, o)
    r = _run(nc, [arrays], core_ids=[0])
    y = np.asarray(r.results[0]["out"])
    return np.ascontiguousarray(y.reshape(P, 8, S).transpose(2, 1, 0).reshape(1, S, 1024))
```

```python
from contextlib import ExitStack

import concourse.bass as bass
import numpy as np
from concourse import mybir

F32 = mybir.dt.float32
F32R = mybir.dt.float32r
ALU = mybir.AluOpType
ACT = mybir.ActivationFunctionType
AX_X = mybir.AxisListType.X

P = 128
S = 512
NT = S // P
EPS = 1e-6
MLA_SCALE = (128 + 64) ** -0.5

CH = 1024
D1 = {"q": 0, "k": 256, "v": 512, "g": 1024, "sb": 1536, "sc": 2048, "sx": 2560, "ca": 3072, "cb": 3584,
      "gate": 4096}
D2 = {"u": 0, "v": 1024, "za": 2048, "cq": 3072, "ckv": 3456, "kr": 3712, "zb": 3776, "xc": 4800, "zc": 6080,
      "gate": 7360}


def fm(name, arr, layer, ks, cols, row=0):
    return (name, [(arr, layer, row + k * P, P, cols) for k in ks])


def rng(a, n=P):
    return (a, a + n)


def lru_tiles(j):
    b0, b1 = (j * P) // 80, (j * P + P - 1) // 80
    return list(range((b0 * 80) // P, (b1 * 80 + 79) // P + 1))


NFULL = 5


def plan():
    out = []
    for l in range(2):
        A = "w_in"

        def one(nm, base, j):
            out.append(fm(f"{nm}{j}", A, l, range(8), rng(base + j * P)))

        for j in range(4):
            one("ca", D1["ca"], j)
            one("cb", D1["cb"], j)
        for j in range(2):
            one("q", D1["q"], j)
            one("k", D1["k"], j)
        for c in range(4):
            out.append((f"v{c}", [(A, l, (2 * c + i) * P, P, rng(D1["v"], 512)) for i in range(2)]))
        for j in range(4):
            one("g", D1["g"], j)
        for j in range(4):
            one("sc", D1["sc"], j)
            one("sx", D1["sx"], j)
            one("sb", D1["sb"], j)
        for b, w in enumerate(("w_ret_out", "w_sc_out", "w_cf_out")):
            one(f"gate{b}_", D1["gate"] + 1024 * b, 0)
            for j in range(8):
                if j < 7:
                    one(f"gate{b}_", D1["gate"] + 1024 * b, j + 1)
                if j % 2 == 0:
                    out.append((f"pr{b}_{j}", [(w, l, k * P, P, rng((j + i) * P)) for i in range(2) for k in range(4)]))
        for j in range(8):
            out.append(fm(f"wo{j}", "w_o", l, range(8), rng(j * P)))
        for j in range(22):
            out.append(fm(f"upg{j}", "w_up", l, range(8), rng(j * P)))
            out.append(fm(f"upv{j}", "w_up", l, range(8), rng(2816 + j * P)))
        for j in [*range(8), *range(NFULL, 8)]:
            for p, ks in enumerate((range(0, 8), range(8, 16), range(16, 22))):
                out.append(fm(f"dn{j}_{p}", "w_down", l, ks, rng(j * P)))
    for l in range(2):
        A = "w_in_2"

        def one(nm, base, j):
            out.append(fm(f"{nm}{j}", A, l, range(8), rng(base + j * P)))

        for j in range(3):
            one("cq", D2["cq"], j)
        for j in range(2):
            one("ckv", D2["ckv"], j)
        out.append(("kr", [(A, l, k * P, P, rng(D2["kr"], 64)) for k in range(8) for _ in range(2)]))
        for h in range(3):
            one("zb", D2["zb"], h)
        for p in range(2):
            out.append((f"qr{p}", [("mla_w_uq_2", l, k * P, P, rng(h * 192 + 128, 64))
                                   for j in (2 * p, 2 * p + 1) for k in range(3) for h in (2 * j, 2 * j + 1)]))
        for p in range(2):
            out.append((f"vb{p}", [("mla_w_ukv_2", l, k * P, P, rng(h * 256 + 128))
                                   for k in range(2) for h in range(4 * p, 4 * p + 4)]))
        for h in range(8):
            out.append((f"qk{h}", [("mla_w_uq_2", l, k * P, P, rng(h * 192)) for k in range(3)]
                        + [("mla_w_ukv_2", l, k * P, P, rng(h * 256)) for k in range(2)]))
            if h < 5:
                one("zb", D2["zb"], h + 3)
            elif h > 5:
                one("gateb_", D2["gate"] + 1024, h - 6)

        def proj(nm, w, nk, b):
            if nm != "b":
                one(f"gate{nm}_", D2["gate"] + 1024 * b, 0)
            for j in range(8):
                if j < 7 and (nm, j) != ("b", 0):
                    one(f"gate{nm}_", D2["gate"] + 1024 * b, j + 1)
                if nk == 8:
                    out.append(fm(f"pr{nm}_{j}", w, l, range(8), rng(j * P)))
                else:
                    out.append(fm(f"pr{nm}_{j}", w, l, range(5), rng(j * P)))
                    out.append(fm(f"pr{nm}_{j}+", w, l, range(5, 10), rng(j * P)))

        for n in range(2):
            for c in range(4):
                out.append((f"va{n}_{c}", [(A, l, (2 * c + i) * P, P, rng(D2["v"] + 512 * n, 512)) for i in range(2)]))
        proj("b", "w_proj_b_2", 8, 1)
        for j in range(8):
            one("u", D2["u"], j)
            one("za", D2["za"], j)
        proj("a", "w_proj_a_2", 8, 0)
        for h in range(2):
            for j in range(5 * h, 5 * h + 5):
                one("xc", D2["xc"], j)
            for j in range(5 * h, 5 * h + 5):
                out.append((f"lru{j}", [(w, l, i, j, "lru") for w in ("lru_w_a_2", "lru_w_x_2") for i in lru_tiles(j)]))
                one("zc", D2["zc"], j)
        proj("c", "w_proj_c_2", 10, 2)
        for j in range(8):
            out.append(fm(f"wo2_{j}", "w_out_2", l, range(8), rng(j * P)))
    return out


def width(chunk):
    return sum(P if p[4] == "lru" else p[4][1] - p[4][0] for p in chunk[1])


def vec_map(items):
    at, out = 0, {}
    for name, n in items:
        out[name] = at
        at += n
    return out, at


V1, NV1 = vec_map([("pre", 8), ("post", 8), ("fpre", 8), ("fpost", 8), ("scw", 12), ("cfw", 124), ("cfb", 4),
                   ("lng", 4), ("lnb", 4), ("fcw", 132)])
V2, NV2 = vec_map([("pre", 8), ("post", 8), ("qg", 3), ("kvg", 2), ("cw", 40), ("cb", 10), ("ba", 10), ("bx", 10),
                   ("lam", 10)])
NV = max(NV1, NV2)


class Engine:

    def __init__(self, e, sem):
        self.e, self.sem, self.n, self.seen = e, sem, 0, {}

    def _wait(self, waits):
        for w in waits:
            if w is None:
                continue
            if isinstance(w, list):
                self._wait(w)
                continue
            sem, value = w
            if self.seen.get(id(sem), 0) < value:
                self.seen[id(sem)] = value
                self.e.wait_ge(sem, value)

    def quiet(self, fn, *waits):
        self._wait(waits)
        fn(self.e)

    def do(self, fn, *waits):
        self._wait(waits)
        self.n += 1
        fn(self.e).then_inc(self.sem, 1)
        return (self.sem, self.n)

    def dma(self, fn, sem, value, *waits):
        self._wait(waits)
        fn(self.e).then_inc(sem, 16)
        return (sem, value)


class Ring:

    def __init__(self, bufs, *toks):
        self.bufs = list(bufs)
        self.idle = [(i, list(toks)) for i in range(len(self.bufs))]

    def take(self):
        i, w = self.idle.pop(0)
        return i, self.bufs[i], w

    def free(self, i, *toks):
        self.idle.append((i, list(toks)))


def build(nc, x_in, wst, vec, cst, tab, gmb, out):
    chunks = plan()
    ctx = ExitStack()
    with ctx:
        def sb(name, shape, dt):
            return ctx.enter_context(nc.sbuf_tensor(name, shape, dt))

        def sem(name):
            return ctx.enter_context(nc.semaphore(name))

        NB = 69
        NRAW, NSP, LA = 4, 4, 2
        base = (nc.sbuf_base + 31) // 32 * 32
        sb("arena", [P, NB * S + 16], F32)
        X = sb("X", [P, 8 * S], F32)
        raw = sb("raw", [P, NRAW, CH], F32)
        wh = sb("wh", [P, NSP, CH], F32R)
        wl = sb("wl", [P, NSP, CH], F32R)
        vt = sb("vt", [P, 2, NV], F32)
        ct = sb("ct", [P, 3, P], F32)
        sm = sb("sm", [P, 160], F32)
        sm2 = sb("sm2", [P, 2, 40], F32)
        ps = ctx.enter_context(nc.psum_tensor("ps", [P, 8, S], F32))
        ident, ones, perm = ct[:, 0, :], ct[:, 1, :], ct[:, 2, :]

        pe, act, dve, pool = (Engine(e, sem("s_" + n)) for e, n in (
            (nc.tensor, "pe"), (nc.scalar, "act"), (nc.vector, "dve"), (nc.gpsimd, "pool")))
        sp = Engine(nc.sync, None)
        s_raw = [sem(f"s_raw{i}") for i in range(NRAW)]
        n_sem = [0]

        def load(eng, dst, src, *waits):
            n_sem[0] += 1
            return eng.dma(lambda e: e.dma_start(dst, src), sem(f"s_ld{n_sem[0]}"), 16, *waits)

        views = {}

        def view(kind, dt, col, n):
            name = f"{kind}{col}_{n}"
            if name not in views:
                views[name] = nc.alloc_sbuf_tensor_at(name, [P, n], dt, offset=base + 4 * col)[:, :]
            return views[name]

        def F(i, n=1):
            return view("f", F32, i * S, n * S)

        def R(i):
            return view("r", F32R, i * S, S)

        def xt(j):
            return X[:, j * S:(j + 1) * S]

        banks = Ring([ps[:, i, :] for i in range(8)])

        class Weights:
            def __init__(self):
                self.loaded = self.cut = self.opened = 0
                self.slots = Ring([(wh[:, i, :], wl[:, i, :]) for i in range(NSP)])
                self.split_tok, self.at, self.kept = {}, {}, {}
                self.share = False
                self.ahead = LA

            def load(self):
                c = self.loaded
                self.loaded += 1
                s = c % NRAW
                w = width(chunks[c])
                sp.dma(lambda e: e.dma_start(raw[:, s, 0:w], wst[c, :, 0:w]), s_raw[s], 16 * (c // NRAW + 1),
                       self.split_tok.get(c - NRAW))

            def keep(self, name, h, l, *toks):
                c = next(c for c in range(self.cut, len(chunks)) if chunks[c][0] == name)
                self.kept[c] = (h, l, list(toks))

            def split(self):
                c = self.cut
                self.cut += 1
                r, w = c % NRAW, width(chunks[c])
                here = (s_raw[r], 16 * (c // NRAW + 1))
                if c in self.kept:
                    h, l, free = self.kept[c]
                    self.at[c] = (None, h, l)
                else:
                    s, (h, l), free = self.slots.take()
                    self.at[c] = (s, h, l)
                a = act.do(lambda e: e.copy(h[:, 0:w], raw[:, r, 0:w]), here, free)
                eng = pool if self.share and c % 2 else dve
                b = eng.do(lambda e: e.tensor_tensor(l[:, 0:w], raw[:, r, 0:w], h[:, 0:w].bitcast(F32),
                                                     ALU.subtract), here, a, free)
                self.split_tok[c] = [a, b]
                if self.loaded < len(chunks):
                    self.load()

            def open(self, name):
                c = self.opened
                assert chunks[c][0] == name, (chunks[c][0], name)
                self.opened += 1
                self.advance(c + self.ahead)
                assert self.cut > c, "a split buffer is still in use"
                pump()
                _, h, l = self.at[c]
                return c, h, l, self.split_tok[c]

            def advance(self, upto):
                while self.cut <= min(upto, len(chunks) - 1) and (self.cut in self.kept or self.slots.idle):
                    self.split()

            def close(self, c, tok):
                if self.at[c][0] is not None:
                    self.slots.free(self.at[c][0], tok)
                self.advance(self.opened - 1 + self.ahead)

        later = []
        early = {}

        def pump():
            if later:
                later.pop(0)()

        def flush():
            while later:
                later.pop(0)()

        W = Weights()

        def mm(o, a, b, start, stop, *waits, sig=False):
            f = lambda e: e.matmul(o, a, b, start=start, stop=stop, skip_group_check=True)
            return pe.do(f, *waits) if sig else pe.quiet(f, *waits)

        def three(o, ah, al, bh, bl, start, stop, *waits, sig=False):
            mm(o, ah, bh, start, False, *waits)
            mm(o, ah, bl, False, False)
            return mm(o, al, bh, False, stop, sig=stop or sig)

        def group(o, ch, cl, cols, xs, waits, start=True, stop=True):
            tok = None
            for i, (c, (xh, xl, xw)) in enumerate(zip(cols, xs)):
                tok = three(o, ch[:, c:c + P], cl[:, c:c + P], xh, xl, start and i == 0,
                            stop and i == len(cols) - 1, waits, xw, sig=i == len(cols) - 1)
            return tok

        def fm_tile(name, xs):
            if name in early:
                return early.pop(name)
            c, h, l, wt = W.open(name)
            i, o, bw = banks.take()
            t = group(o, h, l, [k * P for k in range(len(xs))], xs, [wt, bw])
            W.close(c, t)
            return i, o, t

        def split_tile(f, h, l, *waits):
            a = act.do(lambda e: e.copy(h, f), *waits)
            b = dve.do(lambda e: e.tensor_tensor(l, f, h.bitcast(F32), ALU.subtract), a, *waits)
            return [a, b]

        def rsqrt_cols(accs, D, wacc):
            i, o, bw = banks.take()
            n = 0
            for a in accs:
                for t in range(NT):
                    tok = mm(o[:, n:n + 1], a[:, t * P:(t + 1) * P], ones[:, 0:1], True, True, bw, wacc, consts, sig=True)
                    n += 1
            j, q, sw = small.take()
            k, r, rw = small.take()
            v = dve.do(lambda e: e.tensor_scalar(q[:, 0:n], o[:, 0:n], 1.0 / D, EPS, ALU.mult, ALU.add), tok, sw)
            banks.free(i, v)
            p = pool.do(lambda e: e.tensor_tensor(r[:, 0:n], q[:, 0:n], half[:, 0:n], ALU.pow), v, rw, consts)
            small.free(j, p)
            return k, r, p

        def spread(r, c0, tok):
            i, o, bw = banks.take()
            for t in range(NT):
                tk = mm(o[:, t * P:(t + 1) * P], r[:, c0 + t:c0 + t + 1].to_broadcast([P, P]), ident, True, True, bw,
                        tok, sig=(t == NT - 1))
            return i, o, tk

        def add_squares(tiles, acc, toks, tmp):
            t = None
            for j, f in enumerate(tiles):
                if j == 0:
                    t = act.do(lambda e, f=f: e.activation(acc, f, ACT.Square), toks[j])
                    continue
                i, q, w = tmp.take()
                a = act.do(lambda e, f=f, q=q: e.activation(q, f, ACT.Square), toks[j], w)
                t = pool.do(lambda e, q=q: e.tensor_tensor(acc, acc, q, ALU.add), a, t)
                tmp.free(i, t)
            return t

        half = sm[:, 144:160]
        small = Ring([sm[:, 16 * i:16 * i + 16] for i in range(8)])
        h0 = dve.do(lambda e: e.memset(half, -0.5))
        c0 = load(sp, ct[:, :, :].rearrange("p a b -> p (a b)"), cst)
        xtok = [load(sp, X[:, 2 * j * S:(2 * j + 2) * S], x_in[:, 2 * j * S:(2 * j + 2) * S]) for j in range(4)]
        xtok = [[xtok[j // 2]] * 2 for j in range(8)]
        consts = [h0, c0]
        vtok = [None] * 4
        vtok[0] = load(sp, vt[:, 0, :], vec[0])
        for _ in range(NRAW):
            W.load()

        def norm_steps(tiles, toks, gain, hs, ls, tmp, wfree, D, vw):
            st, res = {}, []

            def squares():
                st["acc"] = tmp.take()
                _, acc, aw = st["acc"]
                st["t"] = add_squares(tiles, acc, [[t, aw] for t in toks], tmp)

            def root():
                ia, acc, _ = st["acc"]
                st["r"] = rsqrt_cols([acc], D, st["t"])
                tmp.free(ia, (pe.sem, pe.n))

            def apply():
                k, r, p = st["r"]
                i, o, tk = spread(r, 0, p)
                small.free(k, tk)
                for j, f in enumerate(tiles):
                    it, q, w = tmp.take()
                    a = dve.do(lambda e: e.scalar_tensor_tensor(
                        out=q, in0=f, scalar=gain[:, j:j + 1], in1=o, op0=ALU.mult, op1=ALU.mult), tk, w, toks[j], vw)
                    s = split_tile(q, hs[j], ls[j], a, wfree)
                    tmp.free(it, *s)
                    res.append((hs[j], ls[j], s))
                banks.free(i, a)

            return [squares, root, apply], res

        def half_cols(hf):
            return slice(256 * hf, 256 * hf + 256)

        class Next:

            def __init__(self, gain, vw, wfree, names):
                self.gain, self.vw, self.wfree, self.names = gain, vw, wfree, names
                self.toks = [[None] * 8, [None] * 8]
                self.open = []

            def xs(self):
                return [(R(j), R(8 + j), [self.toks[0][j], self.toks[1][j]]) for j in range(8)]

            def early_first(self, n, between=()):
                c, h, l, wt = W.open(self.names[n])
                i, o, bw = banks.take()
                cs_ = half_cols(0)
                for k in range(8):
                    for f in between if k == 4 else ():
                        f()
                    w = slice(k * P, (k + 1) * P)
                    three(o[:, cs_], h[:, w], l[:, w], R(k)[:, cs_], R(8 + k)[:, cs_], k == 0, k == 7, wt, bw,
                          self.toks[0][k])
                self.open.append((c, h, l, i, o))

            def early_second(self):
                cs_ = half_cols(1)
                for k in range(8):
                    w = slice(k * P, (k + 1) * P)
                    for n, (c, h, l, i, o) in enumerate(self.open):
                        tk = three(o[:, cs_], h[:, w], l[:, w], R(k)[:, cs_], R(8 + k)[:, cs_], k == 0, k == 7,
                                   self.toks[1][k])
                        if k == 7:
                            early[self.names[n]] = (i, o, tk)
                for n, (c, *_) in enumerate(self.open):
                    W.close(c, early[self.names[n]][2])

        def chain(hf, tmp, nxt, y=None):
            c = half_cols(hf)
            st, head, tail, out_ = {}, [], [], []

            def rsq(D, key):
                j, q, sw = small.take()
                k, r, rw = small.take()
                o = st["cols"][1]
                v = dve.do(lambda e: e.tensor_scalar(q[:, 0:2], o[:, 0:2], 1.0 / D, EPS, ALU.mult, ALU.add),
                           st["ctok"], sw)
                banks.free(st["cols"][0], v)
                p = pool.do(lambda e: e.tensor_tensor(r[:, 0:2], q[:, 0:2], half[:, 0:2], ALU.pow), v, rw, consts)
                small.free(j, p)
                st["r"] = (k, r, p)

            def row():
                k, r, p = st["r"]
                i, o, bw = banks.take()
                for t in range(2):
                    tk = mm(o[:, c.start + t * P:c.start + (t + 1) * P], r[:, t:t + 1].to_broadcast([P, P]), ident,
                            True, True, bw, p, sig=(t == 1))
                small.free(k, tk)
                st["row"] = (i, o, tk)

            def cols_of(f, first, last, *waits):
                if first:
                    i, o, bw = banks.take()
                    st["cols"] = (i, o, bw)
                i, o, bw = st["cols"]
                for t in range(2):
                    tk = mm(o[:, t:t + 1], f[:, c.start + t * P:c.start + (t + 1) * P], ones[:, 0:1],
                            first and t == 0, last, bw, consts, *waits, sig=True)
                st["ctok"] = tk
                return tk

            if y is not None:
                base, acc, acct, ytok = y

                def y_sum():
                    st["acc"] = cols_of(acc, True, True, acct[hf])
                    rsq(1024, "y")

                head += [y_sum, row]

            def update(j):
                if y is not None:
                    i, o, tk = st["row"]
                    yj = F(base + j)
                    a = dve.do(lambda e: e.tensor_tensor(yj[:, c], yj[:, c], o[:, c], ALU.mult), tk, ytok[hf][j])
                    xtok[j][hf] = dve.do(lambda e: e.tensor_tensor(xt(j)[:, c], xt(j)[:, c], yj[:, c], ALU.add), a,
                                         xtok[j])
                    if j == 7:
                        banks.free(i, a)
                if nxt is None:
                    return
                if j == 0:
                    st["sq"] = tmp.take()
                    _, q, w = st["sq"]
                    st["sqt"] = act.do(lambda e: e.activation(q[:, c], xt(j)[:, c], ACT.Square), xtok[j][hf], w)
                    return
                iq, q, w = tmp.take()
                t = act.do(lambda e: e.activation(q[:, c], xt(j)[:, c], ACT.Square), xtok[j][hf], w)
                s = st["sq"][1]
                st["sqt"] = pool.do(lambda e: e.tensor_tensor(s[:, c], s[:, c], q[:, c], ALU.add), t, st["sqt"])
                tmp.free(iq, st["sqt"])

            def x_sum():
                tmp.free(st["sq"][0], cols_of(st["sq"][1], True, True, st["sqt"]))
                rsq(1024, "x")

            def h_tiles(js):
                i, o, tk = st["row"]
                parts = []
                for j in js:
                    iq, q, w = tmp.take()
                    a = dve.do(lambda e: e.scalar_tensor_tensor(
                        out=q[:, c], in0=xt(j)[:, c], scalar=nxt.gain[:, j:j + 1], in1=o[:, c], op0=ALU.mult,
                        op1=ALU.mult), tk, w, xtok[j][hf], nxt.vw)
                    b = act.do(lambda e: e.copy(R(j)[:, c], q[:, c]), a, nxt.wfree)
                    parts.append((j, iq, q, a, b))
                for j, iq, q, a, b in parts:
                    eng = pool if j % 2 else dve
                    d = eng.do(lambda e: e.tensor_tensor(R(8 + j)[:, c], q[:, c], R(j)[:, c].bitcast(F32),
                                                         ALU.subtract), a, b, nxt.wfree)
                    tmp.free(iq, b, d)
                    nxt.toks[hf][j] = [b, d]
                    if j == 7:
                        banks.free(i, a)

            def some(f, js):
                return lambda: [f(j) for j in js]

            pairs = [(0, 1), (2, 3), (4, 5), (6, 7)]
            ups = [some(update, js) for js in pairs]
            if nxt is not None:
                tail += [x_sum, row]
                out_ += [lambda js=js: h_tiles(js) for js in pairs]
            return head, ups, tail, out_

        def finish_halves(parts, nxt):
            head, ups, tail, out_ = parts
            if nxt is None:
                flush()
                for f in head + ups:
                    f()
                return
            while len(later) > 2:
                later.pop(0)()
            head[0]()
            W.share = False
            W.advance(W.opened + 2)
            W.ahead = 0
            flush()
            nxt.early_first(0, head[1:] + ups[:2])
            nxt.early_first(1, ups[2:])
            nxt.early_first(2)
            for f in tail + out_:
                f()
            W.ahead = LA
            W.advance(W.opened - 1 + LA)
            nxt.early_second()

        def boundary(tile, nfull, wait, ybase, gain, tmp, wy, vw, nxt):
            ia, acc, aw = tmp.take()
            acct, ytok = [None, None], [[None] * 8, [None] * 8]

            def evacuate(j, hfs, c, i, o, tk):
                y = F(ybase + j)
                a = act.do(lambda e: e.activation(y[:, c], o[:, c], ACT.Copy, scale=gain[:, j:j + 1]), tk, wy, vw)
                if acct[hfs[0]] is None:
                    b = t = act.do(lambda e: e.activation(acc[:, c], o[:, c], ACT.Square), tk, aw)
                else:
                    iq, q, w = tmp.take()
                    b = act.do(lambda e: e.activation(q[:, c], o[:, c], ACT.Square), tk, w)
                    t = dve.do(lambda e: e.tensor_tensor(acc[:, c], acc[:, c], q[:, c], ALU.add), b, acct)
                    tmp.free(iq, t)
                banks.free(i, b)
                for hf in hfs:
                    acct[hf], ytok[hf][j] = t, a

            for j in range(nfull):
                evacuate(j, (0, 1), slice(0, S), *tile(j, None))
            flush()
            for hf in range(2):
                for j in range(nfull, 8):
                    evacuate(j, (hf,), half_cols(hf), *tile(j, hf))
                parts = chain(hf, tmp, nxt, (ybase, acc, acct, ytok))
                if hf == 0:
                    head, ups, tail, out_ = parts
                    later.extend([lambda: None] + head + ups + [lambda: None] * wait + tail + out_)
                    W.share = True
                else:
                    finish_halves(parts, nxt)
                    W.share = False
            tmp.free(ia, (pe.sem, pe.n))

        def ring_tile(names, xs_):
            def tile(j, hf):
                i, o, bw = banks.take()
                c = slice(0, S) if hf is None else half_cols(hf)
                parts = names(j)
                for n, (name, ks) in enumerate(parts):
                    m, h, l, wt = W.open(name)
                    for some in (range(0, 4), range(4, len(ks))):
                        if hf == 1 and some[0]:
                            pump()
                        tk = group(o[:, c], h, l, [k * P for k in some],
                                   [(xs_[ks[k]][0][:, c], xs_[ks[k]][1][:, c], xs_[ks[k]][2]) for k in some], [wt, bw],
                                   n == 0 and some[0] == 0, n == len(parts) - 1 and some[0] > 0)
                    W.close(m, tk)
                return i, o, tk
            return tile

        def kept_tile(name, nfull, xs_, places, *free):
            for j in range(nfull, 7):
                h, l = (view("r", F32R, i * S, CH) for i in places[j - nfull])
                W.keep(f"{name}{j}", h, l, *free)
            mine = {}

            def tile(j, hf):
                c = slice(0, S) if hf is None else half_cols(hf)
                if hf != 1:
                    mine[j] = W.open(f"{name}{j}")
                m, h, l, wt = mine[j]
                i, o, bw = banks.take()
                for k0 in (0, 4):
                    if hf == 1:
                        pump()
                    tk = group(o[:, c], h, l, [k * P for k in range(k0, k0 + 4)],
                               [(xs_[k][0][:, c], xs_[k][1][:, c], xs_[k][2]) for k in range(k0, k0 + 4)], [wt, bw],
                               k0 == 0, k0 == 4)
                if (hf == 1) == (j == 7):
                    W.close(m, tk)
                return i, o, tk
            return tile

        def gate_proj(b, gname, pname, ys, M, tmp, xs, wm, kind, done=None):
            pr = None
            gates = [fm_tile(f"gate{gname}_0", xs)]
            for j in range(8):
                if j < 7:
                    gates.append(fm_tile(f"gate{gname}_{j + 1}", xs))
                ig, og, tg = gates[j]
                if kind == "pair":
                    if j % 2 == 0:
                        pr = W.open(f"pr{pname}_{j}")
                    ip, op, bw = banks.take()
                    c, h, l, wt = pr
                    tp = group(op, h, l, [(j % 2 * 4 + k) * P for k in range(4)], ys, [wt, bw])
                    if j % 2:
                        W.close(c, tp)
                else:
                    ip, op, bw = banks.take()
                    n = len(ys) if len(ys) == 8 else 5
                    for k0 in range(0, len(ys), n):
                        c, h, l, wt = W.open(f"pr{pname}_{j}" + ("+" if k0 else ""))
                        tp = group(op, h, l, [k * P for k in range(n)], ys[k0:k0 + n], [wt, bw], k0 == 0,
                                   k0 + n == len(ys))
                        W.close(c, tp)
                it, q, w = tmp.take()
                a = act.do(lambda e, q=q, og=og: e.activation(q, og, ACT.Sigmoid), tg, w)
                banks.free(ig, a)
                if b == 0:
                    m = dve.do(lambda e, q=q, op=op, j=j: e.tensor_tensor(F(M + j), q, op, ALU.mult), a, tp, wm)
                    mtok[j] = [m]
                    banks.free(ip, m)
                    tmp.free(it, m)
                else:
                    m = dve.do(lambda e, q=q, op=op: e.tensor_tensor(q, q, op, ALU.mult), a, tp)
                    banks.free(ip, m)
                    g = pool.do(lambda e, q=q, j=j: e.tensor_tensor(F(M + j), F(M + j), q, ALU.add), m, mtok[j])
                    mtok[j] = [g]
                    tmp.free(it, g)
                if done and j:
                    done(j - 1)
            if done:
                done(7)
            return tp

        mtok = [None] * 8

        def rope(i, o, tk, dst, cosF, sinF, tmp, *waits):
            iq, q, w = tmp.take()
            a = act.do(lambda e: e.copy(q, o), tk, w)
            banks.free(i, a)
            b = pool.do(lambda e: e.tensor_tensor(dst, q, cosF, ALU.mult), a, *waits)

            def rotate():
                ir, r, bw = banks.take()
                tr = mm(r, perm, q, True, True, a, bw, consts, sig=True)
                c = dve.do(lambda e: e.tensor_tensor(q, r, sinF, ALU.mult), tr, b, *waits)
                banks.free(ir, c)
                d = pool.do(lambda e: e.tensor_tensor(dst, dst, q, ALU.add), c, b)
                tmp.free(iq, d)
                return d

            return rotate

        def mark():
            return [(e.sem, e.n) for e in (pe, act, dve, pool)]

        tri = [0, 512, 896, 1152]

        def vc1(l, name, n=0):
            return vt[:, l, V1[name] + n:]

        def vc2(l, name, n=0):
            return vt[:, l, V2[name] + n:]

        NAMES1, NAMES2 = ["ca0", "cb0", "ca1"], ["cq0", "cq1", "cq2"]
        nxt = Next(vc1(0, "pre"), vtok[0], None, NAMES1)
        temps = Ring([F(i) for i in range(62, 69)])
        first, second = chain(0, temps, nxt), chain(1, temps, nxt)
        for f in first[1]:
            f()
        W.advance(1)
        for f in first[2]:
            f()
        for f, g in zip(first[3], second[1]):
            f()
            g()
        nxt.early_first(0)
        second[2][0]()
        nxt.early_first(1, second[2][1:] + second[3])
        nxt.early_first(2)
        nxt.early_second()

        for l in range(2):
            vi = l % 2
            v = vt[:, vi, :]
            vw = vtok[l]
            temps = Ring([F(i) for i in range(62, 69)])
            start = mark() if l else []

            def vc(name, n=0):
                return v[:, V1[name] + n:]

            H, L = [R(j) for j in range(8)], [R(8 + j) for j in range(8)]
            xs = nxt.xs()
            cs = [load(pool, F(52 + i), tab[:, i * S:(i + 1) * S], start) for i in range(2)]
            dec = [load(pool, F(54 + i), tab[:, (2 + i) * S:(3 + i) * S], start) for i in range(4)]
            vtok[l + 1] = load(pool, vt[:, 1 - vi, :], vec[l + 1], start)

            gtok = []
            for j in range(4):
                ia, oa, ta = fm_tile(f"ca{j}", xs)
                ib, ob, tb = fm_tile(f"cb{j}", xs)
                it, q, w = temps.take()
                a = act.do(lambda e: e.activation(q, ob, ACT.Sigmoid), tb, w)
                banks.free(ib, a)
                g = dve.do(lambda e: e.tensor_tensor(F(16 + j), q, oa, ALU.mult), a, ta, start)
                banks.free(ia, g)
                temps.free(it, g)
                gtok.append(g)
            ctok = [None] * 4

            def tap(k, j):
                G, C = F(16 + j), F(20 + j)
                w = vc("cfw", 31 * j + k)
                s = 30 - k
                if s == 0:
                    ctok[j] = act.do(lambda e: e.activation(C, G, ACT.Identity, bias=vc("cfb", j)[:, 0:1],
                                                            scale=w[:, 0:1]), gtok[j], vw, start)
                else:
                    ctok[j] = dve.do(lambda e: e.scalar_tensor_tensor(
                        out=C[:, s:S], in0=G[:, 0:S - s], scalar=w[:, 0:1], in1=C[:, s:S], op0=ALU.mult,
                        op1=ALU.add), ctok[j])

            for k in range(30, -1, -1):
                later.append(lambda k=k: [tap(k, j) for j in range(4)])

            QK = []
            for j in range(2):
                for m, nm in enumerate("qk"):
                    i, o, tk = fm_tile(f"{nm}{j}", xs)
                    if m or j:
                        QK.append(turn_())
                    turn_ = rope(i, o, tk, F(48 + 2 * m + j), F(52), F(53), temps, cs, start)
            vb = [banks.take() for _ in range(NT)]
            for c in range(4):
                n, h, lo, wt = W.open(f"v{c}")
                for t in range(NT):
                    for i in range(2):
                        k = 2 * c + i
                        ts = slice(t * P, (t + 1) * P)
                        tk = three(vb[t][1], H[k][:, ts], L[k][:, ts], h[:, i * S:(i + 1) * S],
                                   lo[:, i * S:(i + 1) * S], k == 0, k == 7, wt, vb[t][2], xs[k][2],
                                   sig=i == 1)
                    if c == 3:
                        a = act.do(lambda e, t=t: e.copy(F(58 + t), vb[t][1]), tk, start)
                        banks.free(vb[t][0], a)
                        if t == 0:
                            V = []
                        V.append(a)
                W.close(n, tk)
                if c == 0:
                    QK.append(turn_())
            sg = []
            otok, sq = [], []
            Sb = Ring([view("f", F32, 24 * S + 1280 * i, 1280) for i in range(2)], start)
            def centre(h):
                im, m, bw = banks.take()
                tm = mm(m, ones, F(40 + h), True, True, bw, ot[h], sig=True)
                oc = dve.do(lambda e: e.scalar_tensor_tensor(out=F(40 + h), in0=m, scalar=-1.0 / P, in1=F(40 + h),
                                                             op0=ALU.mult, op1=ALU.add), tm)
                banks.free(im, oc)
                otok.append(oc)

            ot = []
            for h in range(4):
                ig, og, tg = fm_tile(f"g{h}", xs)
                if h:
                    centre(h - 1)
                it, q, w = temps.take()
                a = act.do(lambda e: e.activation(q, og, ACT.Sigmoid), tg, w)
                b = dve.do(lambda e: e.tensor_tensor(F(44 + h), q, og, ALU.mult), a, start)
                temps.free(it, b)
                banks.free(ig, b)
                sg.append(b)
                pr = slice(64 * (h % 2), 64 * (h % 2) + 64)
                si, sbuf, sw = Sb.take()
                st = []
                for i in range(NT):
                    ib, o, bw = banks.take()
                    n = S - P * i
                    tk = mm(o[:, 0:n], F(50 + h // 2)[pr, i * P:(i + 1) * P], F(48 + h // 2)[pr, i * P:S], True, True,
                            bw, QK, sig=True)
                    st.append(dve.do(lambda e, o=o, n=n, i=i: e.tensor_tensor(
                        sbuf[:, tri[i]:tri[i] + n], o[:, 0:n], F(54 + h)[:, 0:n], ALU.mult), tk, sw, dec))
                    banks.free(ib, st[-1])
                io, o, bw = banks.take()
                for i in range(NT):
                    tk = mm(o[:, i * P:S], F(58 + i)[:, h * P:(h + 1) * P], sbuf[:, tri[i]:tri[i] + S - P * i], i == 0,
                            i == NT - 1, bw, V, st[i], sig=(i == NT - 1))
                Sb.free(si, tk)
                ot.append(act.do(lambda e: e.copy(F(40 + h), o), tk, start))
                banks.free(io, ot[h])
            ret_done = [(pe.sem, pe.n), (dve.sem, dve.n)]
            sqt, ret = [], {}
            Yret = []

            def ret_squares():
                for h in range(4):
                    it, q, w = temps.take()
                    sqt.append((it, q, act.do(lambda e: e.activation(q, F(40 + h), ACT.Square), otok[h], w)))

            def ret_root():
                ret["r"] = rsqrt_cols([q for _, q, _ in sqt], P, [t for _, _, t in sqt])
                for it, _, _ in sqt:
                    temps.free(it, (pe.sem, pe.n))

            def ret_out(h):
                kk, r, p = ret["r"]
                i, o, tk = spread(r, 4 * h, p)
                it, q, w = temps.take()
                a = pool.do(lambda e: e.tensor_tensor(q, F(40 + h), F(44 + h), ALU.mult), w, otok[h], sg[h])
                b = dve.do(lambda e: e.tensor_tensor(q, q, o, ALU.mult), a, tk)
                banks.free(i, b)
                s = split_tile(q, R(40 + h), R(44 + h), b)
                temps.free(it, *s)
                Yret.append((R(40 + h), R(44 + h), s))
                if h == 3:
                    small.free(kk, tk)

            for n, f in enumerate([lambda: None, lambda: centre(3), ret_squares, ret_root] + [lambda h=h: ret_out(h) for h in range(4)]):
                g = later[n]
                later[n] = lambda f=f, g=g: (f(), g())

            Ysc = []
            for j in range(4):
                ic, oc, tc = fm_tile(f"sc{j}", xs)
                it, q, w = temps.take()
                a = act.do(lambda e: e.copy(q, oc), tc, w)
                banks.free(ic, a)
                ix, ox, tx = fm_tile(f"sx{j}", xs)
                b = dve.do(lambda e: e.tensor_tensor(q, q, ox, ALU.mult), a, tx)
                banks.free(ix, b)
                iu, u, w = temps.take()
                cw = vc("scw", 3 * j)
                t = act.do(lambda e: e.activation(u, q, ACT.Copy, scale=cw[:, 2:3]), b, w, vw)
                for s in (1, 2):
                    t = dve.do(lambda e, s=s: e.scalar_tensor_tensor(
                        out=u[:, s:S], in0=q[:, 0:S - s], scalar=cw[:, 2 - s:3 - s], in1=u[:, s:S], op0=ALU.mult,
                        op1=ALU.add), t)
                temps.free(it, t)
                ib, ob, tb = fm_tile(f"sb{j}", xs)
                t = dve.do(lambda e: e.tensor_tensor(u, u, ob, ALU.mult), t, tb)
                banks.free(ib, t)
                s = split_tile(u, R(32 + j), R(36 + j), t, start)
                temps.free(iu, *s)
                Ysc.append((R(32 + j), R(36 + j), s))

            M = 48
            tp = gate_proj(0, "0", "0", Yret, M, temps, xs, ret_done, "pair")

            ln = {}

            def ln_sum():
                ln["acc"] = temps.take()
                ia, acc, aw = ln["acc"]
                t = pool.do(lambda e: e.tensor_tensor(acc, F(20), F(21), ALU.add), ctok, aw)
                for j in (2, 3):
                    t = pool.do(lambda e: e.tensor_tensor(acc, acc, F(20 + j), ALU.add), t)
                ln["t"] = t

            def ln_centre():
                im, m, bw = banks.take()
                tm = mm(m, ones, ln["acc"][1], True, True, bw, ln["t"], sig=True)
                t = [dve.do(lambda e: e.scalar_tensor_tensor(out=F(20 + j), in0=m, scalar=-1.0 / 512, in1=F(20 + j),
                                                             op0=ALU.mult, op1=ALU.add), tm) for j in range(4)]
                banks.free(im, t[-1])
                ln["t"] = add_squares([F(20 + j) for j in range(4)], ln["acc"][1], [[q, tm] for q in t], temps)

            def ln_rsqrt():
                ln["r"] = rsqrt_cols([ln["acc"][1]], 512, ln["t"])
                temps.free(ln["acc"][0], (pe.sem, pe.n))

            def ln_spread():
                kk, r, p = ln["r"]
                ln["o"] = spread(r, 0, p)
                small.free(kk, ln["o"][2])

            Ycf = []

            def ln_out(j):
                i, o, tk = ln["o"]
                C = F(20 + j)
                a = dve.do(lambda e: e.scalar_tensor_tensor(out=C, in0=C, scalar=vc("lng", j)[:, 0:1], in1=o,
                                                            op0=ALU.mult, op1=ALU.mult), tk)
                if j == 3:
                    banks.free(i, a)
                it, q, w = temps.take()
                b = act.do(lambda e: e.activation(q, C, ACT.Sigmoid, bias=vc("lnb", j)[:, 0:1]), a, w)
                c = dve.do(lambda e: e.scalar_tensor_tensor(out=q, in0=C, scalar=vc("lnb", j)[:, 0:1], in1=q,
                                                            op0=ALU.add, op1=ALU.mult), b)
                s = split_tile(q, R(24 + j), R(28 + j), c, ret_done)
                temps.free(it, *s)
                Ycf.append((R(24 + j), R(28 + j), s))

            later += [ln_sum, lambda: None, ln_centre, lambda: None, lambda: None, ln_rsqrt, ln_spread]
            later += [lambda j=j: ln_out(j) for j in range(4)]
            tp1 = gate_proj(1, "1", "1", Ysc, M, temps, xs, None, "pair")
            flush()
            ms = []

            def cut_merged(j):
                s = split_tile(F(M + j), R(32 + j), R(40 + j), mtok[j], tp1)
                ms.append((R(32 + j), R(40 + j), s))

            tp2 = gate_proj(2, "2", "2", Ycf, M, temps, xs, None, "pair", cut_merged)
            nxt = Next(vc("fpre"), vw, tp2, ["upg0", "upv0", "upg1"])
            boundary(kept_tile("wo", 2, ms, [(16, 18), (20, 22), (48, 50), (52, 54), (56, 58)], mark()), 2, 3, 24, vc("post"), temps, tp2, vw, nxt)

            xs = nxt.xs()
            ff = mark()
            temps = Ring([F(i) for i in range(60, 69)], ff)
            Fs = []
            for j in range(22):
                gv = []
                for m, nm in enumerate(("upg", "upv")):
                    i, o, tk = fm_tile(f"{nm}{j}", xs)
                    it, q, w = temps.take()
                    cw = vc("fcw", 3 * (22 * m + j))
                    t = act.do(lambda e: e.activation(q, o, ACT.Copy, scale=cw[:, 2:3]), tk, w)
                    for s in (1, 2):
                        t = dve.do(lambda e, s=s: e.scalar_tensor_tensor(
                            out=q[:, s:S], in0=o[:, 0:S - s], scalar=cw[:, 2 - s:3 - s], in1=q[:, s:S], op0=ALU.mult,
                            op1=ALU.add), t)
                    banks.free(i, t)
                    gv.append((it, q, t))
                (ig, g, tg), (iv, u, tu) = gv
                it, q, w = temps.take()
                a = act.do(lambda e: e.activation(q, g, ACT.Sigmoid), tg, w)
                b = pool.do(lambda e: e.tensor_tensor(u, g, u, ALU.mult), tg, tu)
                c = dve.do(lambda e: e.tensor_tensor(q, q, u, ALU.mult), a, b)
                temps.free(ig, a, b)
                temps.free(iv, c)
                s = split_tile(q, R(16 + j), R(38 + j), c, ff)
                temps.free(it, *s)
                Fs.append((R(16 + j), R(38 + j), s))

            up_done = (pe.sem, pe.n)
            if l == 0:
                nxt = Next(vc1(1, "pre"), vtok[1], up_done, NAMES1)
            else:
                nxt = Next(vc2(0, "pre"), vtok[2], up_done, NAMES2)
            boundary(ring_tile(lambda j: [(f"dn{j}_{p}", ks) for p, ks in enumerate(
                (range(0, 8), range(8, 16), range(16, 22)))], Fs), NFULL, 4, 0, vc("fpost"), temps, up_done, vw, nxt)

        for l in range(2):
            vi = l % 2
            v = vt[:, vi, :]
            vw = vtok[2 + l]
            start = mark()
            temps = Ring([F(i) for i in list(range(61, 69)) + [46, 52, 53, 54, 55, 56, 57, 58]], start)

            def vc(name, n=0):
                return v[:, V2[name] + n:]

            H, L = [R(j) for j in range(8)], [R(8 + j) for j in range(8)]
            xs = nxt.xs()
            cs = [load(pool, F(59 + i), tab[:, i * S:(i + 1) * S], start) for i in range(2)]
            if l == 0:
                vtok[3] = load(pool, vt[:, 1, :], vec[3], start)

            lam = vc("lam")[:, 0:10]
            q = [small.take() for _ in range(5)]
            u, d, z, z2, pp = (a[1][:, 0:10] for a in q)
            cc = sm2[:, vi, :]
            w5 = [a[2] for a in q]
            t = act.do(lambda e: e.activation(u, lam, ACT.Abs), vw, w5)
            t = act.do(lambda e: e.activation(u, u, ACT.Exp, scale=-1.0), t)
            t = dve.do(lambda e: e.tensor_scalar(d, u, 2.0, None, ALU.add), t, w5)
            t = dve.do(lambda e: e.reciprocal(d, d), t)
            t = dve.do(lambda e: e.tensor_tensor(z, u, d, ALU.mult), t)
            t = dve.do(lambda e: e.tensor_tensor(z2, z, z, ALU.mult), t)
            t = dve.do(lambda e: e.tensor_scalar(pp, z2, 1.0 / 17, None, ALU.mult), t)
            for n in (15, 13, 11, 9, 7, 5, 3):
                t = dve.do(lambda e, n=n: e.scalar_tensor_tensor(out=pp, in0=pp, scalar=1.0 / n, in1=z2, op0=ALU.add,
                                                                 op1=ALU.mult), t)
            t = dve.do(lambda e: e.scalar_tensor_tensor(out=pp, in0=pp, scalar=1.0, in1=z, op0=ALU.add, op1=ALU.mult), t)
            t = dve.do(lambda e: e.tensor_scalar(d, lam, -1.0, 0.0, ALU.mult, ALU.max), t)
            t = dve.do(lambda e: e.scalar_tensor_tensor(out=d, in0=pp, scalar=2.0, in1=d, op0=ALU.mult, op1=ALU.add), t)
            t = dve.do(lambda e: e.tensor_scalar(cc[:, 0:10], d, -4.0, None, ALU.mult), t, start)
            t = dve.do(lambda e: e.tensor_scalar(cc[:, 10:20], d, -8.0, None, ALU.mult), t)
            t = dve.do(lambda e: e.tensor_scalar(cc[:, 20:40], vc("ba")[:, 0:20], 0.5, None, ALU.mult), t)
            cctok = t
            for a in q:
                small.free(a[0], t)

            cqt, kvt = [], []
            for j in range(3):
                i, o, tk = fm_tile(f"cq{j}", xs)
                cqt.append(act.do(lambda e: e.copy(F(47 + j), o), tk, start))
                banks.free(i, cqt[-1])
            steps, qs = norm_steps([F(47 + j) for j in range(3)], cqt, vc("qg"), [R(32 + j) for j in range(3)],
                                   [R(35 + j) for j in range(3)], temps, start, 384, vw)
            later.extend(steps)
            for j in range(2):
                i, o, tk = fm_tile(f"ckv{j}", xs)
                kvt.append(act.do(lambda e: e.copy(F(50 + j), o), tk, start))
                banks.free(i, kvt[-1])
            i, o, tk = fm_tile("kr", xs)
            turn_kr = rope(i, o, tk, F(42), F(59), F(60), temps, cs, start)
            steps, kvs = norm_steps([F(50 + j) for j in range(2)], kvt, vc("kvg"), [R(38 + j) for j in range(2)],
                                    [R(40 + j) for j in range(2)], temps, start, 256, vw)
            later.extend(steps)

            zs, zdone = [], []

            def gate_head(h):
                z = F((20, 21, 22, 23, 29, 30, 31, 67)[h])
                iz, oz, tz = fm_tile(f"zb{h}", xs)
                s = act.do(lambda e: e.activation(z, oz, ACT.Tanh, scale=0.5), tz, start if h < 7 else head0)
                s2 = dve.do(lambda e: e.scalar_tensor_tensor(out=z, in0=z, scalar=1.0, in1=oz, op0=ALU.add,
                                                             op1=ALU.mult), s)
                banks.free(iz, s2)
                zs.append((z, s2))

            gate_head(0)
            krt = turn_kr()
            gate_head(1)
            gate_head(2)
            flush()
            raw_free = mark()
            qrt = []
            for p in range(2):
                c, h, lo, wt = W.open(f"qr{p}")
                for j in range(2):
                    i, o, bw = banks.take()
                    tk = group(o, h, lo, [(3 * j + k) * P for k in range(3)], qs, [wt, bw])
                    if p or j:
                        qrt.append(turn_())
                    turn_ = rope(i, o, tk, F(43 + 2 * p + j), F(59), F(60), temps, cs, start,
                                 raw_free if 2 * p + j == 3 else None)
                W.close(c, tk)
            V = []
            for n in range(2):
                c, h, lo, wt = W.open(f"vb{n}")
                for t in range(NT):
                    ib, o, bw = banks.take()
                    ts = slice(t * P, (t + 1) * P)
                    for k in range(2):
                        tk = three(o, kvs[k][0][:, ts], kvs[k][1][:, ts], h[:, k * S:(k + 1) * S],
                                   lo[:, k * S:(k + 1) * S], k == 0, k == 1, wt, bw, kvs[k][2])
                    a = act.do(lambda e: e.copy(F(47 + 4 * n + t), o), tk, raw_free, mark())
                    banks.free(ib, a)
                    V.append(a)
                    if n == 0 and t == 0:
                        qrt.append(turn_())
                W.close(c, tk)
            head0 = mark()
            qkr = Ring([(F(55), F(56)), (F(57), F(58))], head0)
            PT = Ring([view("f", F32, 59 * S + 1280 * i, 1280) for i in range(2)], head0)
            Pb = Ring([view("f", F32, 64 * S, 1280)], head0)

            ahead = {}

            def pre(h):
                c, wh_, wl_, wt = W.open(f"qk{h}")
                b, (qn, kn), w = qkr.take()
                i, o, bw = banks.take()
                tq = group(o, wh_, wl_, [k * P for k in range(3)], qs, [wt, bw])
                a = act.do(lambda e: e.copy(qn, o), tq, w)
                banks.free(i, a)
                i2, o2, bw = banks.take()
                tk = group(o2, wh_, wl_, [(3 + k) * P for k in range(2)], kvs, [wt, bw])
                W.close(c, tk)
                d = dve.do(lambda e: e.tensor_copy(kn, o2), tk, w)
                banks.free(i2, d)
                if h < 5:
                    gate_head(h + 3)
                elif h > 5:
                    ahead[f"gateb_{h - 6}"] = fm_tile(f"gateb_{h - 6}", xs)
                return b, qn, kn, [a, d]

            def scores(h, pr):
                b, qn, kn, tk0 = pr
                rows = slice(64 * (h % 2), 64 * (h % 2) + 64)
                ip, pb, pw = Pb.take()
                im, mx, mw = small.take()
                ir, rs, rw = small.take()
                bk, mt = [], []
                for i in range(NT):
                    n = (i + 1) * P
                    ib, o, bw = banks.take()
                    mm(o[:, 0:n], qn[:, i * P:n], kn[:, 0:n], True, False, bw, tk0)
                    tk = mm(o[:, 0:n], F(43 + h // 2)[rows, i * P:n], F(42)[rows, 0:n], False, True, qrt, krt, sig=True)
                    t = dve.do(lambda e, o=o, i=i: e.memset(o[0:64, i * P + 64:(i + 1) * P], -1e30), tk)
                    t = dve.do(lambda e, o=o, i=i, n=n: e.tensor_reduce(mx[:, i:i + 1], o[:, 0:n], AX_X, ALU.max), t, mw)
                    bk.append((ib, o, n))
                    mt.append(t)
                qkr.free(b, tk)
                nb = dve.do(lambda e: e.tensor_scalar(mx[:, 4:8], mx[:, 0:4], -MLA_SCALE, None, ALU.mult), mt)
                ex = []
                offs = [0, 128, 384, 768]
                for i, (ib, o, n) in enumerate(bk):
                    a = act.do(lambda e, o=o, i=i, n=n: e.activation(
                        pb[:, offs[i]:offs[i] + n], o[:, 0:n], ACT.Exp, bias=mx[:, 4 + i:5 + i], scale=MLA_SCALE,
                        accum_out=rs[:, i:i + 1]), nb, pw, rw)
                    banks.free(ib, a)
                    ex.append(a)
                small.free(im, a)
                t = dve.do(lambda e: e.reciprocal(rs[:, 4:8], rs[:, 0:4]), ex)
                nt = []
                for i in range(NT):
                    n = (i + 1) * P
                    nt.append(dve.do(lambda e, i=i, n=n: e.tensor_scalar(
                        pb[:, offs[i]:offs[i] + n], pb[:, offs[i]:offs[i] + n], rs[:, 4 + i:5 + i], None, ALU.mult), t))
                small.free(ir, nt[-1])
                return ip, pb, offs, nt

            def turn(h, pr):
                ip, pb, offs, nt = pr
                it, pt, tw = PT.take()
                ev = []
                for a, ms_ in enumerate(((0,), (1,), (2, 3))):
                    ib, o, bw = banks.take()
                    c = 0
                    for m in ms_:
                        for i in range(m, NT):
                            dst = o[:, c:c + P]
                            src = pb[:, offs[i] + m * P:offs[i] + (m + 1) * P]
                            tk = pe.do(lambda e, dst=dst, src=src: e.transpose(dst, src, ident), bw, nt[i], consts)
                            c += P
                    f = (lambda e, o=o, c=c, a=a: e.tensor_copy(pt[:, tri[a]:tri[a] + c], o[:, 0:c]))
                    g = (lambda e, o=o, c=c, a=a: e.copy(pt[:, tri[a]:tri[a] + c], o[:, 0:c]))
                    ev.append(dve.do(f, tk, tw) if a == 0 else act.do(g, tk, tw))
                    banks.free(ib, ev[-1])
                Pb.free(ip, tk)
                return it, pt, ev

            Yb = []

            def values(h, tr):
                it, pt, ev = tr
                io, o, bw = banks.take()
                for i in range(NT):
                    tk = mm(o[:, i * P:S], F(47 + 4 * (h // 4) + i)[:, (h % 4) * P:(h % 4 + 1) * P],
                            pt[:, tri[i]:tri[i] + S - i * P], i == 0, i == NT - 1, bw, V, ev, sig=(i == NT - 1))
                PT.free(it, tk)
                z, zt = zs[h]
                t = dve.do(lambda e: e.scalar_tensor_tensor(out=z, in0=z, scalar=0.5, in1=o, op0=ALU.mult,
                                                            op1=ALU.mult), tk, zt)
                banks.free(io, t)
                s = split_tile(z, R(16 + h), R(24 + h), t, start, zdone)
                zdone.append(s)
                Yb.append((R(16 + h), R(24 + h), s))

            cur = pre(0)
            sc = scores(0, cur)
            for h in range(8):
                nxt = pre(h + 1) if h < 7 else None
                tr = turn(h, sc)
                sc = scores(h + 1, nxt) if h < 7 else None
                values(h, tr)
                cur = nxt
            early.update(ahead)

            M = 56
            att = mark()
            temps = Ring([F(i) for i in [64, 65, 66, 67, 68] + list(range(46, 56))], att)
            gb = [load(pool, F(40 + 2 * i, 2), gmb[l, :, 2 * i * S:(2 * i + 2) * S], att) for i in range(2)]
            ws = [load(pool, F(44 + i), gmb[l, :, (4 + i) * S:(5 + i) * S], att) for i in range(2)]
            zm = dve.do(lambda e: e.memset(F(44)[64:128, :].rearrange("p (g i) -> p g i", g=4)[:, :, 0:64], 0.0), ws)
            lnt = []
            for n in range(2):
                vb = [banks.take() for _ in range(NT)]
                for c in range(4):
                    m, h, lo, wt = W.open(f"va{n}_{c}")
                    for t in range(NT):
                        for i in range(2):
                            k = 2 * c + i
                            ts = slice(t * P, (t + 1) * P)
                            tk = three(vb[t][1], H[k][:, ts], L[k][:, ts], h[:, i * S:(i + 1) * S],
                                       lo[:, i * S:(i + 1) * S], k == 0, k == 7, wt, vb[t][2], xs[k][2],
                                   sig=i == 1)
                        if c == 3:
                            a = act.do(lambda e, t=t, n=n: e.copy(F(32 + 2 * t, 2)[:, n * S:(n + 1) * S], vb[t][1]), tk, att)
                            banks.free(vb[t][0], a)
                            lnt.append(a)
                    W.close(m, tk)
            Va = []

            def layer_norm(t):
                ist, st, sw = small.take()
                imv, mv, mw = small.take()
                vv = F(32 + 2 * t, 2)
                a = dve.do(lambda e: e.bn_stats(st[:, 0:6], vv[:, 0:S]), lnt[t], lnt[4 + t], sw)
                b = dve.do(lambda e: e.bn_stats(st[:, 6:12], vv[:, S:2 * S]), a)
                b = dve.do(lambda e: e.bn_aggr(mv[:, 0:2], st[:, 0:12]), a, b, mw)
                small.free(ist, b)
                b = dve.do(lambda e: e.tensor_scalar(mv[:, 2:3], mv[:, 1:2], EPS, None, ALU.add), b)
                r = pool.do(lambda e: e.tensor_tensor(mv[:, 3:4], mv[:, 2:3], half[:, 0:1], ALU.pow), b)
                c = dve.do(lambda e: e.scalar_tensor_tensor(out=vv, in0=vv, scalar=mv[:, 0:1], in1=F(40, 2),
                                                            op0=ALU.subtract, op1=ALU.mult), b, gb)
                c = dve.do(lambda e: e.scalar_tensor_tensor(out=vv, in0=vv, scalar=mv[:, 3:4], in1=F(42, 2),
                                                            op0=ALU.mult, op1=ALU.add), c, r)
                small.free(imv, c)
                Va.append(c)

            later += [lambda t=t: layer_norm(t) for t in range(NT)]
            tpb = gate_proj(0, "b", "b", Yb, M, temps, xs, att, "one")
            Ya = []
            uz = []

            def both_gates(j):
                uz.append((fm_tile(f"u{j}", xs), fm_tile(f"za{j}", xs)))

            both_gates(0)
            for j in range(8):
                if j < 7:
                    both_gates(j + 1)
                (iu, ou, tu), (iz, oz, tz) = uz[j]
                io, o, bw = banks.take()
                g = j // 2
                for b in range(NT):
                    tk = mm(o[:, b * P:(b + 1) * P], F(32 + 2 * b, 2)[:, j * P:(j + 1) * P],
                            F(44)[:, g * P:(g + 1) * P], True, True, bw, Va, ws, zm, sig=(b == NT - 1))
                it, q, w = temps.take()
                i2, q2, w2 = temps.take()
                bs = F(45)[:, g * P:(g + 1) * P].unsqueeze(1).to_broadcast([P, NT, P])
                a = dve.do(lambda e: e.tensor_tensor(q[:, :].rearrange("p (b i) -> p b i", b=NT),
                                                     o[:, :].rearrange("p (b i) -> p b i", b=NT), bs, ALU.add),
                           tk, w, ws)
                banks.free(io, a)
                a = dve.do(lambda e: e.tensor_tensor(q, q, ou, ALU.mult), a, tu)
                banks.free(iu, a)
                s = act.do(lambda e: e.activation(q2, oz, ACT.Sigmoid), tz, w2)
                s = dve.do(lambda e: e.tensor_tensor(q2, q2, oz, ALU.mult), s)
                banks.free(iz, s)
                a = pool.do(lambda e: e.tensor_tensor(q, q, q2, ALU.mult), a, s)
                temps.free(i2, a)
                s = split_tile(q, R(16 + j), R(24 + j), a, tpb)
                temps.free(it, *s)
                Ya.append((R(16 + j), R(24 + j), s))
            gate_proj(1, "a", "a", Ya, M, temps, xs, None, "one")

            lru = mark()
            temps = Ring([F(i) for i in [52, 53, 54, 55, 64, 65, 66, 67, 68]], lru)
            Yc = []
            half_done = lru
            for hf in range(2):
                xcs = {}
                for t in range(5):
                    j = 5 * hf + t
                    i, o, tk = fm_tile(f"xc{j}", xs)
                    x_ = F(16 + t)
                    cw = vc("cw", 4 * j)
                    a = act.do(lambda e: e.activation(x_, o, ACT.Identity, bias=vc("cb", j)[:, 0:1],
                                                      scale=cw[:, 3:4]), tk, half_done, vw)
                    for s in (1, 2, 3):
                        a = dve.do(lambda e, s=s: e.scalar_tensor_tensor(
                            out=x_[:, s:S], in0=o[:, 0:S - s], scalar=cw[:, 3 - s:4 - s], in1=x_[:, s:S],
                            op0=ALU.mult, op1=ALU.add), a)
                    banks.free(i, a)
                    s = split_tile(x_, R(21 + t), R(26 + t), a, half_done)
                    xcs[j] = (R(21 + t), R(26 + t), s)
                def gates(t):
                    j = 5 * hf + t
                    ks = lru_tiles(j)
                    c, h, lo, wt = W.open(f"lru{j}")
                    ia, oa, bw = banks.take()
                    ta = group(oa, h, lo, [k * P for k in range(len(ks))], [xcs[k] for k in ks], [wt, bw])
                    ii, oi, bw = banks.take()
                    ti = group(oi, h, lo, [(len(ks) + k) * P for k in range(len(ks))], [xcs[k] for k in ks], [wt, bw])
                    W.close(c, ti)
                    iz, oz, tz = fm_tile(f"zc{j}", xs)
                    n1, r, w1 = temps.take()
                    n2, q, w2 = temps.take()
                    n3, a_, w3 = temps.take()
                    n4, z, w4 = temps.take()
                    a = act.do(lambda e: e.activation(r, oa, ACT.Tanh, scale=0.5, bias=cc[:, 20 + j:21 + j]), ta, w1,
                               cctok)
                    banks.free(ia, a)
                    b = act.do(lambda e: e.activation(q, oi, ACT.Tanh, scale=0.5, bias=cc[:, 30 + j:31 + j]), ti, w2)
                    banks.free(ii, b)
                    ea = act.do(lambda e: e.activation(a_, r, ACT.Exp, scale=cc[:, j:j + 1], bias=cc[:, j:j + 1]), a, w3)
                    e2 = act.do(lambda e: e.activation(r, r, ACT.Exp, scale=cc[:, 10 + j:11 + j],
                                                       bias=cc[:, 10 + j:11 + j]), ea)
                    sz = act.do(lambda e: e.activation(z, oz, ACT.Tanh, scale=0.5), tz, w4)
                    d = dve.do(lambda e: e.tensor_scalar(r, r, 1.0, None, ALU.min), e2)
                    q_ = dve.do(lambda e: e.scalar_tensor_tensor(out=q, in0=q, scalar=1.0, in1=F(16 + t), op0=ALU.add,
                                                                 op1=ALU.mult), b)
                    sz = dve.do(lambda e: e.scalar_tensor_tensor(out=z, in0=z, scalar=1.0, in1=oz, op0=ALU.add,
                                                                 op1=ALU.mult), sz)
                    banks.free(iz, sz)
                    return j, (n1, n2, n3, n4), (r, q, a_, z), d, q_, ea, sz

                def recur(j, n, bufs, d, q_, ea, sz):
                    r, q, a_, z = bufs
                    d = act.do(lambda e: e.activation(r, r, ACT.Sqrt, scale=-1.0, bias=1.0), d)
                    yield
                    d = dve.do(lambda e: e.scalar_tensor_tensor(out=r, in0=r, scalar=0.5, in1=q, op0=ALU.mult,
                                                                op1=ALU.mult), d, q_)
                    d = dve.do(lambda e: e.tensor_tensor_scan(q, a_, r, 0.0, ALU.mult, ALU.add), d, ea)
                    temps.free(n[0], d)
                    temps.free(n[2], d)
                    d = dve.do(lambda e: e.scalar_tensor_tensor(out=q, in0=q, scalar=0.5, in1=z, op0=ALU.mult,
                                                                op1=ALU.mult), d, sz)
                    temps.free(n[3], d)
                    yield
                    s = split_tile(q, R(32 + j), R(42 + j), d, lru)
                    temps.free(n[1], *s)
                    Yc.append((R(32 + j), R(42 + j), s))
                    yield

                two = []
                for ts_ in ((0, 1), (2, 3), (4,)):
                    last, two = two, []
                    for t in ts_:
                        two.append(recur(*gates(t)))
                        for g in last:
                            next(g)
                        last = []
                    for _ in range(2):
                        for g in two:
                            next(g)
                for g in two:
                    next(g)
                half_done = mark()
            ms = []

            def cut_merged(j):
                s = split_tile(F(M + j), R(16 + j), R(24 + j), mtok[j], half_done)
                ms.append((R(16 + j), R(24 + j), s))

            tpc = gate_proj(2, "c", "c", Yc, M, temps, xs, None, "one", cut_merged)
            nxt = Next(vc2(1, "pre"), vtok[3], tpc, NAMES2) if l == 0 else None
            boundary(kept_tile("wo2_", 2, ms, [(40, 42), (44, 46), (48, 50), (56, 58), (60, 62)], mark()), 2, 3, 32, vc("post"), temps, tpc, vw, nxt)

        s_out = sem("s_out")
        for j in range(8):
            sp.dma(lambda e, j=j: e.dma_start(out[:, j * S:(j + 1) * S], xt(j)), s_out, 16 * (j + 1), xtok[j])
        nc.sync.wait_ge(s_out, 16 * 8)


def pack_weights(a):
    chunks = plan()
    out = np.zeros((len(chunks), P, CH), np.float32)
    dense = {}
    for w in ("lru_w_a_2", "lru_w_x_2"):
        d = np.zeros((2, 1280, 1280), np.float32)
        for b in range(16):
            d[:, 80 * b:80 * b + 80, 80 * b:80 * b + 80] = a[w][:, b]
        dense[w] = d
    for n, (_, pieces) in enumerate(chunks):
        c = 0
        for p in pieces:
            if p[4] == "lru":
                w, l, i, j, _ = p
                out[n, :, c:c + P] = dense[w][l, i * P:(i + 1) * P, j * P:(j + 1) * P]
                c += P
            else:
                w, l, r, nr, (c0, c1) = p
                out[n, 0:nr, c:c + c1 - c0] = a[w][l, r:r + nr, c0:c1]
                c += c1 - c0
    return out


def cols(x):
    return x.reshape(-1, P).T


def taps(w):
    k = w.shape[0]
    return w.reshape(k, -1, P).transpose(2, 1, 0).reshape(P, -1)


def pack_vectors(a):
    out = np.zeros((4, P, NV), np.float32)
    for l in range(2):
        for m, parts in ((V1, {"pre": cols(a["norm_mix_pre"][l]), "post": cols(a["norm_mix_post"][l]),
                               "fpre": cols(a["norm_ffn_pre"][l]), "fpost": cols(a["norm_ffn_post"][l]),
                               "scw": taps(a["sc_conv_w"][l]), "cfw": taps(a["cf_conv_w"][l]),
                               "cfb": cols(a["cf_conv_b"][l]), "lng": cols(a["cf_ln_g"][l]),
                               "lnb": cols(a["cf_ln_b"][l]), "fcw": taps(a["ffn_conv_w"][l])}),
                         (V2, {"pre": cols(a["pre_norm_g_2"][l]), "post": cols(a["post_norm_g_2"][l]),
                               "qg": cols(a["mla_q_norm_g_2"][l]), "kvg": cols(a["mla_kv_norm_g_2"][l]),
                               "cw": taps(a["lru_conv_w_2"][l]), "cb": cols(a["lru_conv_b_2"][l]),
                               "ba": cols(a["lru_b_a_2"][l]), "bx": cols(a["lru_b_x_2"][l]),
                               "lam": cols(a["lru_lambda_2"][l])})):
            for name, v in parts.items():
                out[l + (2 if m is V2 else 0), :, m[name]:m[name] + v.shape[1]] = v
    return out


def pack_spatial(a):
    out = np.zeros((2, P, 6 * S), np.float32)
    for l in range(2):
        out[l, :, 0:1024] = np.broadcast_to(a["gm_ln_g_2"][l], (P, 1024))
        out[l, :, 1024:2048] = np.broadcast_to(a["gm_ln_b_2"][l], (P, 1024))
        out[l, :, 2048:2560] = a["gm_ws_2"][l].transpose(2, 0, 1).reshape(P, 512)
        out[l, :, 2560:3072] = np.broadcast_to(a["gm_bs_2"][l].reshape(-1), (P, 512))
    return out


def constants():
    c = np.zeros((P, 3, P), np.float32)
    c[:, 0] = np.eye(P)
    c[:, 1] = 1.0
    for m in range(P):
        if m % 64 < 32:
            c[m + 32, 2, m] = -1.0
        else:
            c[m - 32, 2, m] = 1.0
    t = np.zeros((P, 6, S), np.float32)
    inv = (np.float32(10000.0) ** (-np.arange(32, dtype=np.float32) / np.float32(32))).astype(np.float32)
    ang = np.arange(S, dtype=np.float32)[None, :] * inv[np.arange(P) % 32][:, None]
    t[:, 0] = np.cos(ang)
    t[:, 1] = np.sin(ang)
    diff = np.arange(S)[None, :] - np.arange(P)[:, None]
    for h in range(4):
        lg = np.log(1.0 - 2.0 ** (-5.0 - h))
        t[:, 2 + h] = np.where(diff >= 0, np.exp(np.maximum(diff, 0) * lg), 0.0) * 64 ** -0.5
    return c.reshape(P, 3 * P), t.reshape(P, 6 * S)


def kernel(**inputs):
    import concourse.bacc as _bacc
    from concourse.bass_utils import run_bass_kernel_spmd as _run

    a = {k: np.asarray(v) for k, v in inputs.items()}
    cst, tab = constants()
    arrays = {
        "x_in": np.ascontiguousarray(a["x"][0].T.reshape(8, P, S).transpose(1, 0, 2).reshape(P, 8 * S)),
        "wst": pack_weights(a),
        "vec": pack_vectors(a),
        "cst": cst,
        "tab": tab,
        "gmb": pack_spatial(a),
    }
    nc = _bacc.Bacc("TRN2", target_bir_lowering=False, num_devices=1)
    args = [nc.dram_tensor(n, v.shape, F32, kind="ExternalInput").ap() for n, v in arrays.items()]
    o = nc.dram_tensor("out", (P, 8 * S), F32, kind="ExternalOutput").ap()
    build(nc, *args, o)
    r = _run(nc, [arrays], core_ids=[0])
    y = np.asarray(r.results[0]["out"])
    return np.ascontiguousarray(y.reshape(P, 8, S).transpose(2, 1, 0).reshape(1, S, 1024))
```
